# Optimizing a Trainium2 kernel written in Bass

```python
import math
import jax, jax.numpy as jnp
from jax import lax
import numpy as np

D_MODEL = 1024
BATCH = 1
SEQ = 256
DEPTH = 2

GRID_W = 64
CTX_LEN = 256
N_HEADS_A = 4
DH_A = 64
DV_A = 2 * DH_A
WIDTH_A = N_HEADS_A * DV_A
N_HEADS_B = 4
DK_B = 64
DV_B = 64
WIDTH_BK = N_HEADS_B * DK_B
WIDTH_B = N_HEADS_B * DV_B
FN_GROUPS = 4
FN_GROUP_DIM = 64
WIDTH_C = FN_GROUPS * FN_GROUP_DIM
MIX_WIDTH = WIDTH_A + WIDTH_B + WIDTH_C
PROJ_SIZES = (WIDTH_A, WIDTH_A, WIDTH_A, WIDTH_BK, WIDTH_BK, WIDTH_BK, WIDTH_B, WIDTH_B, WIDTH_C)
PROJ_WIDTH = 3 * WIDTH_A + 3 * WIDTH_BK + 2 * WIDTH_B + WIDTH_C
D_FF = 2816
CONV_W = 3
Q_BLOCK = 128
CHUNK = 64
ROPE_BASE = 10000.0
EPS = 1e-6


def rms_norm(x, w):
    xf = x.astype(jnp.float32)
    y = xf * lax.rsqrt(jnp.mean(xf * xf, axis=-1, keepdims=True) + EPS)
    return (y * w.astype(jnp.float32)).astype(x.dtype)

def modulate(h, shift, scale):
    return h * (1 + scale) + shift

def flip(a):
    return jnp.flip(a, axis=1)

def axial_rope(rows):
    pos_r = jnp.repeat(jnp.arange(rows), GRID_W).astype(jnp.float32)
    pos_c = jnp.tile(jnp.arange(GRID_W), rows).astype(jnp.float32)
    half = DH_A // 2
    inv_freq = ROPE_BASE ** (-jnp.arange(0, half, 2, dtype=jnp.float32) / half)
    ang_r = pos_r[:, None] * inv_freq
    ang_c = pos_c[:, None] * inv_freq
    ang = jnp.concatenate([ang_r, ang_r, ang_c, ang_c], axis=-1)
    return jnp.cos(ang), jnp.sin(ang)

def _rotate_half(p):
    h = p.shape[-1] // 2
    return jnp.concatenate([-p[..., h:], p[..., :h]], axis=-1)

def apply_axial_rope(t, cos, sin):
    t_row, t_col = jnp.split(t, 2, axis=-1)
    rot = jnp.concatenate([_rotate_half(t_row), _rotate_half(t_col)], axis=-1)
    cos = cos[None, :, None, None, :]
    sin = sin[None, :, None, None, :]
    return (t * cos + rot * sin).astype(t.dtype)

def diff_attend(q, k, v, lam):
    s = jnp.einsum('bqhcd,bkhcd->bhcqk', q, k).astype(jnp.float32) * (DH_A ** -0.5)
    p = jax.nn.softmax(s, axis=-1)
    a = p[:, :, 0] - lam * p[:, :, 1]
    return jnp.einsum('bhqk,bkhd->bqhd', a, v.astype(jnp.float32))

def diff_attend_blocks(q, k, v, lam):
    b, l = q.shape[:2]
    nb = l // Q_BLOCK
    qb = q.reshape(b, nb, Q_BLOCK, N_HEADS_A, 2, DH_A).transpose(1, 0, 2, 3, 4, 5)
    o = lax.map(lambda blk: diff_attend(blk, k, v, lam), qb)
    return o.transpose(1, 0, 2, 3, 4).reshape(b, l, N_HEADS_A, DV_A)

def diff_head_norm(o, w, lam_init):
    b, l = o.shape[:2]
    return (rms_norm(o, w) * (1.0 - lam_init)).reshape(b, l, WIDTH_A)

def log_forget(z, lb):
    zf = z.astype(jnp.float32)
    return jnp.logaddexp(jnp.log(lb), jnp.log1p(-lb) + jax.nn.log_sigmoid(zf))

def hgrn_scan(q, k, v, logf, s0):
    b, l, h, _ = q.shape
    dv = v.shape[-1]
    nc = l // CHUNK

    def chunks(a):
        return a.reshape(b, nc, CHUNK, h, a.shape[-1]).transpose(1, 0, 3, 2, 4)

    lower = jnp.tril(jnp.ones((CHUNK, CHUNK), dtype=bool))[:, :, None]

    def step(state, blk):
        qc, kc, vc, gc = blk
        cum = jnp.cumsum(gc, axis=2)
        rel = jnp.where(lower, cum[:, :, :, None, :] - cum[:, :, None, :, :], -jnp.inf)
        scores = jnp.einsum('bhtd,bhsd,bhtsd->bhts', qc, kc, jnp.exp(rel))
        o = (jnp.einsum('bhts,bhsv->bhtv', scores, vc)
             + jnp.einsum('bhtd,bhdv->bhtv', qc * jnp.exp(cum), state))
        cum_end = cum[:, :, -1:, :]
        state = (jnp.exp(cum_end)[:, :, 0, :, None] * state
                 + jnp.einsum('bhsd,bhsv->bhdv', kc * jnp.exp(cum_end - cum), vc))
        return state, o

    state, o = lax.scan(step, s0, (chunks(q), chunks(k), chunks(v), chunks(logf)))
    return o.transpose(1, 0, 3, 2, 4).reshape(b, l, h, dv), state

def hgrn_final_state(k, v, logf):
    tail = flip(jnp.cumsum(flip(logf), axis=1)) - logf
    return jnp.einsum('blhk,blhv->bhkv', k * jnp.exp(tail), v)

def hgrn_bidir(m, s_fwd, s_bwd):
    o_f, st_f = hgrn_scan(m['qh'], m['kf'], m['vh'], m['gf'], s_fwd)
    o_b, st_b = hgrn_scan(flip(m['qh']), flip(m['kb']), flip(m['vh']), flip(m['gb']), s_bwd)
    return o_f + flip(o_b), st_f, st_b

def hgrn_out(o, og, w):
    b, l = o.shape[:2]
    return (rms_norm(o, w) * jax.nn.silu(og.astype(jnp.float32))).reshape(b, l, WIDTH_B)

def fourier_mix(u, w):
    b, l, _ = u.shape
    ug = u.astype(jnp.float32).reshape(b, l, FN_GROUPS, FN_GROUP_DIM)
    y = jnp.fft.fft2(ug, axes=(1, 3), norm='ortho').real.reshape(b, l, WIDTH_C)
    return y.astype(u.dtype) @ w

def conv_ffn(h, w_up, conv_w, conv_b, w_down):
    u = h @ w_up
    up = jnp.pad(u, ((0, 0), (1, 1), (0, 0)))
    u = up[:, :-2] * conv_w[0] + up[:, 1:-1] * conv_w[1] + up[:, 2:] * conv_w[2] + conv_b
    gate, val = jnp.split(u, 2, axis=-1)
    return (jax.nn.silu(gate) * val) @ w_down

def unpack(p, lb):
    b, l, _ = p.shape
    idx = np.cumsum(PROJ_SIZES)[:-1].tolist()
    qa, ka, va, qh, zf, zb, ih, gh, uf = jnp.split(p, idx, axis=-1)
    gf = log_forget(zf, lb[0]).reshape(b, l, N_HEADS_B, DK_B)
    gb = log_forget(zb, lb[1]).reshape(b, l, N_HEADS_B, DK_B)
    return {
        'qa': qa.reshape(b, l, N_HEADS_A, 2, DH_A),
        'ka': ka.reshape(b, l, N_HEADS_A, 2, DH_A),
        'va': va.reshape(b, l, N_HEADS_A, DV_A),
        'qh': qh.reshape(b, l, N_HEADS_B, DK_B).astype(jnp.float32),
        'gf': gf, 'gb': gb,
        'kf': -jnp.expm1(gf), 'kb': -jnp.expm1(gb),
        'vh': ih.reshape(b, l, N_HEADS_B, DV_B).astype(jnp.float32),
        'og': gh.reshape(b, l, N_HEADS_B, DV_B),
        'uf': uf,
    }

def merge(att, rec, four, w_out, dt):
    return jnp.concatenate([att.astype(dt), rec.astype(dt), four.astype(dt)], axis=-1) @ w_out

def first_inputs(seed: int = 0) -> dict:
    key = jax.random.key(seed)
    ks = jax.random.split(key, 20)
    f32 = jnp.float32

    def nrm(k, shape, s):
        return s * jax.random.normal(k, shape, f32)

    return {
        'x': nrm(ks[0], (BATCH, SEQ, D_MODEL), 1.0),
        'c': nrm(ks[1], (BATCH, D_MODEL), 1.0),
        'ctx': nrm(ks[2], (BATCH, CTX_LEN, D_MODEL), 1.0),
        'c_ctx': nrm(ks[3], (D_MODEL,), 1.0),
        'w_ada': nrm(ks[4], (DEPTH, D_MODEL, 6 * D_MODEL), 0.5 * D_MODEL ** -0.5),
        'b_ada': nrm(ks[5], (DEPTH, 6 * D_MODEL), 0.02),
        'norm1_w': 1.0 + nrm(ks[6], (DEPTH, D_MODEL), 0.05),
        'norm2_w': 1.0 + nrm(ks[7], (DEPTH, D_MODEL), 0.05),
        'w_in': nrm(ks[8], (DEPTH, D_MODEL, PROJ_WIDTH), D_MODEL ** -0.5),
        'lam_qk': nrm(ks[9], (DEPTH, 4, DH_A), 0.1),
        'subln_w': 1.0 + nrm(ks[10], (DEPTH, DV_A), 0.05),
        'lb_param': nrm(ks[11], (DEPTH, 2, WIDTH_BK), 0.5),
        'hgrn_norm_w': 1.0 + nrm(ks[12], (DEPTH, DV_B), 0.05),
        'w_fnet': nrm(ks[13], (DEPTH, WIDTH_C, WIDTH_C), WIDTH_C ** -0.5),
        'w_out': nrm(ks[14], (DEPTH, MIX_WIDTH, D_MODEL), MIX_WIDTH ** -0.5),
        'w_up': nrm(ks[15], (DEPTH, D_MODEL, 2 * D_FF), D_MODEL ** -0.5),
        'conv_w': jnp.array([0.0, 1.0, 0.0], f32)[None, :, None] + nrm(ks[16], (DEPTH, CONV_W, 2 * D_FF), 0.2),
        'conv_b': nrm(ks[17], (DEPTH, 2 * D_FF), 0.02),
        'w_down': nrm(ks[18], (DEPTH, D_FF, D_MODEL), D_FF ** -0.5),
        'final_norm_w': 1.0 + nrm(ks[19], (D_MODEL,), 0.05),
    }

def first_block(x, c, ctx, c_ctx, w_ada, b_ada, norm1_w, norm2_w, w_in, lam_qk, subln_w,
              lb_param, hgrn_norm_w, w_fnet, w_out, w_up, conv_w, conv_b, w_down, final_norm_w):
    b, l, _ = x.shape
    rows = l // GRID_W
    cos, sin = axial_rope(rows)
    lb_all = jnp.cumsum(jax.nn.softmax(lb_param.astype(jnp.float32), axis=0), axis=0)
    lb_all = lb_all - lb_all[0:1]
    c_act = jax.nn.silu(c)
    cc_act = jax.nn.silu(c_ctx)
    xc = ctx
    for li in range(DEPTH):
        last = li == DEPTH - 1
        dt = x.dtype
        mod = c_act @ w_ada[li] + b_ada[li]
        sh1, sc1, g1, sh2, sc2, g2 = jnp.split(mod[:, None, :], 6, axis=-1)
        mod_c = cc_act @ w_ada[li] + b_ada[li]
        sh1c, sc1c, g1c, sh2c, sc2c, g2c = jnp.split(mod_c[None, None, :], 6, axis=-1)
        lam_init = 0.8 - 0.6 * math.exp(-0.3 * li)
        lq1, lk1, lq2, lk2 = lam_qk[li].astype(jnp.float32)
        lam = jnp.exp(jnp.sum(lq1 * lk1)) - jnp.exp(jnp.sum(lq2 * lk2)) + lam_init

        m = unpack(modulate(rms_norm(x, norm1_w[li]), sh1, sc1) @ w_in[li], lb_all[li])
        mc = unpack(modulate(rms_norm(xc, norm1_w[li]), sh1c, sc1c) @ w_in[li], lb_all[li])

        k_all = jnp.concatenate([mc['ka'], apply_axial_rope(m['ka'], cos, sin)], axis=1)
        v_all = jnp.concatenate([mc['va'], m['va']], axis=1)
        att = diff_head_norm(diff_attend_blocks(apply_axial_rope(m['qa'], cos, sin), k_all, v_all, lam),
                             subln_w[li], lam_init)

        if last:
            s_f = hgrn_final_state(mc['kf'], mc['vh'], mc['gf'])
            s_b = hgrn_final_state(flip(mc['kb']), flip(mc['vh']), flip(mc['gb']))
        else:
            zeros = jnp.zeros((xc.shape[0], N_HEADS_B, DK_B, DV_B), jnp.float32)
            o_c, s_f, s_b = hgrn_bidir(mc, zeros, zeros)
        o_l, _, _ = hgrn_bidir(m, s_f, s_b)
        rec = hgrn_out(o_l, m['og'], hgrn_norm_w[li])

        four = fourier_mix(m['uf'], w_fnet[li])

        x = x + g1 * merge(att, rec, four, w_out[li], dt)
        x = x + g2 * conv_ffn(modulate(rms_norm(x, norm2_w[li]), sh2, sc2),
                              w_up[li], conv_w[li], conv_b[li], w_down[li])

        if not last:
            att_c = diff_head_norm(diff_attend(mc['qa'], mc['ka'], mc['va'], lam), subln_w[li], lam_init)
            rec_c = hgrn_out(o_c, mc['og'], hgrn_norm_w[li])
            four_c = fourier_mix(mc['uf'], w_fnet[li])
            xc = xc + g1c * merge(att_c, rec_c, four_c, w_out[li], dt)
            xc = xc + g2c * conv_ffn(modulate(rms_norm(xc, norm2_w[li]), sh2c, sc2c),
                                     w_up[li], conv_w[li], conv_b[li], w_down[li])
    return rms_norm(x, final_norm_w)


HEAD_DIM = 64
NORM_EPS = 1e-6

RWKV_HEADS = 8
RWKV_WIDTH = RWKV_HEADS * HEAD_DIM
RWKV_DECAY_RANK = 64
RWKV_ICLR_RANK = 64
RWKV_GATE_RANK = 128
RWKV_GN_EPS = 64e-5

NSA_Q_HEADS = 8
NSA_KV_GROUPS = 2
NSA_CMP_LEN = 32
NSA_CMP_STRIDE = 16
NSA_CMP_HIDDEN = 256
NSA_SEL_BLOCK = 64
NSA_SEL_TOPN = 16
NSA_WINDOW = 512
NSA_FORCE_SCORE = 1e9

SWA_Q_HEADS = 8
SWA_KV_HEADS = 2
SWA_WINDOW = 128

REL_BUCKETS = 32
REL_MAX_DIST = 128

PEER_HEADS = 8
PEER_NKEYS = 128
PEER_EXPERTS = PEER_NKEYS * PEER_NKEYS
PEER_QDIM = 256
PEER_TOPK = 16
PEER_TOK_BLOCK = 128

RWKV_SPLITS = (RWKV_WIDTH, RWKV_WIDTH, RWKV_WIDTH, RWKV_DECAY_RANK, RWKV_ICLR_RANK, RWKV_GATE_RANK)
NSA_SPLITS = (NSA_Q_HEADS * HEAD_DIM,) + (NSA_KV_GROUPS * HEAD_DIM,) * 6 + (NSA_Q_HEADS * 3,)
SWA_SPLITS = (SWA_Q_HEADS * HEAD_DIM, SWA_KV_HEADS * HEAD_DIM, SWA_KV_HEADS * HEAD_DIM)
GATE_SPLITS = (D_MODEL, D_MODEL, D_MODEL)
RWKV_COLS = sum(RWKV_SPLITS)
IN_SPLITS = RWKV_SPLITS + NSA_SPLITS + SWA_SPLITS + GATE_SPLITS
IN_COLS = sum(IN_SPLITS)


def split_cols(z, sizes):
    cuts = [int(c) for c in np.cumsum(sizes)[:-1]]
    return jnp.split(z, cuts, axis=-1)

def rmsnorm(x, w):
    xf = x.astype(jnp.float32)
    y = xf * lax.rsqrt(jnp.mean(xf * xf, axis=-1, keepdims=True) + NORM_EPS)
    return (y * w.astype(jnp.float32)).astype(x.dtype)

def token_shift(z, mu):
    z_prev = jnp.pad(z, ((0, 0), (1, 0), (0, 0)))[:, :-1]
    return z + mu * (z_prev - z)

def t5_bucket(dist):
    n = jnp.maximum(dist, 0)
    max_exact = REL_BUCKETS // 2
    nf = jnp.maximum(n, max_exact).astype(jnp.float32)
    large = max_exact + (jnp.log(nf / max_exact) / math.log(REL_MAX_DIST / max_exact)
                         * (REL_BUCKETS - max_exact)).astype(jnp.int32)
    large = jnp.minimum(large, REL_BUCKETS - 1)
    return jnp.where(n < max_exact, n, large)

def masked_softmax(s, mask):
    s = jnp.where(mask, s.astype(jnp.float32), -jnp.inf)
    m = jnp.max(s, axis=-1, keepdims=True)
    m = jnp.where(jnp.isfinite(m), m, 0.0)
    e = jnp.exp(s - m)
    return e / jnp.maximum(jnp.sum(e, axis=-1, keepdims=True), 1e-30)

def sink_softmax(s, mask, sink):
    s = jnp.where(mask, s.astype(jnp.float32), -jnp.inf)
    sink = sink.astype(jnp.float32)[None, :, :, None, None]
    m = jnp.maximum(jnp.max(s, axis=-1, keepdims=True), sink)
    e = jnp.exp(s - m)
    return e / (jnp.sum(e, axis=-1, keepdims=True) + jnp.exp(sink - m))

def rwkv7_mixer(zr, zk, zv, zw, za, zg, w0, w2, a0, a2, g2, k_k, k_a, r_k, ln_w, ln_b):
    B, S, C = zr.shape
    H, N = RWKV_HEADS, HEAD_DIM
    f32 = jnp.float32
    log_w = -jax.nn.softplus(-(w0 + jnp.tanh(zw) @ w2)) - 0.5
    decay = jnp.exp(-jnp.exp(log_w.astype(f32)))
    a = jax.nn.sigmoid(a0 + za @ a2)
    g = jax.nn.sigmoid(zg) @ g2
    kk = (zk * k_k).reshape(B, S, H, N).astype(f32)
    kk = kk * lax.rsqrt(jnp.maximum(jnp.sum(kk * kk, axis=-1, keepdims=True), 1e-12))
    k = zk * (1.0 + (a - 1.0) * k_a)
    hd = lambda z: z.reshape(B, S, H, N).astype(f32)
    r_h, k_h, v_h, a_h, w_h = hd(zr), hd(k), hd(zv), hd(a), hd(decay)
    tm = lambda z: jnp.swapaxes(z, 0, 1)

    def step(state, inp):
        r_t, w_t, k_t, v_t, kk_t, a_t = inp
        sa = jnp.einsum('bhij,bhj->bhi', state, -kk_t)
        state = (state * w_t[:, :, None, :] + sa[..., None] * (kk_t * a_t)[:, :, None, :]
                 + v_t[..., None] * k_t[:, :, None, :])
        return state, jnp.einsum('bhij,bhj->bhi', state, r_t)

    s0 = jnp.zeros((B, H, N, N), f32)
    _, y = lax.scan(step, s0, (tm(r_h), tm(w_h), tm(k_h), tm(v_h), tm(kk), tm(a_h)))
    y = tm(y)
    mu = jnp.mean(y, axis=-1, keepdims=True)
    var = jnp.mean(jnp.square(y - mu), axis=-1, keepdims=True)
    y = ((y - mu) * lax.rsqrt(var + RWKV_GN_EPS)).reshape(B, S, C) * ln_w + ln_b
    bonus = jnp.sum(r_h * k_h * r_k, axis=-1, keepdims=True) * v_h
    out = (y + bonus.reshape(B, S, C)) * g
    return out.astype(zr.dtype)

def nsa_compress(z, pe, w1, w2):
    B, S, G, dh = z.shape
    n_sub = NSA_CMP_LEN // NSA_CMP_STRIDE
    chunks = z.reshape(B, S // NSA_CMP_STRIDE, NSA_CMP_STRIDE, G, dh)
    n_cmp = S // NSA_CMP_STRIDE - n_sub + 1
    blocks = jnp.concatenate([chunks[:, j:j + n_cmp] for j in range(n_sub)], axis=2)
    blocks = blocks + pe[None, None, :, None, :]
    flat = blocks.transpose(0, 3, 1, 2, 4).reshape(B, G, n_cmp, NSA_CMP_LEN * dh)
    return jax.nn.gelu(flat @ w1, approximate=False) @ w2

def nsa_mixer(q, kc, vc, ks, vs, kw, vw, gates, pe_k, pe_v, ck_w1, ck_w2, cv_w1, cv_w2, bias_tbl):
    B, S, _ = q.shape
    G, Hg, dh = NSA_KV_GROUPS, NSA_Q_HEADS // NSA_KV_GROUPS, HEAD_DIM
    scale = dh ** -0.5
    heads = lambda z: z.reshape(B, S, G, dh)
    kv_t = lambda z: heads(z).transpose(0, 2, 1, 3)
    qh = q.reshape(B, S, G, Hg, dh).transpose(0, 2, 3, 1, 4)
    gh = jax.nn.sigmoid(gates.reshape(B, S, G, Hg, 3)).transpose(0, 2, 3, 1, 4)

    k_cmp = nsa_compress(heads(kc), pe_k, ck_w1, ck_w2)
    v_cmp = nsa_compress(heads(vc), pe_v, cv_w1, cv_w2)
    n_cmp = k_cmp.shape[2]
    cmp_start = jnp.arange(n_cmp) * NSA_CMP_STRIDE
    cmp_end = cmp_start + NSA_CMP_LEN - 1
    n_sel = S // NSA_SEL_BLOCK
    sel_start = jnp.arange(n_sel) * NSA_SEL_BLOCK
    overlap = ((cmp_end[:, None] >= sel_start[None, :])
               & (cmp_start[:, None] <= sel_start[None, :] + NSA_SEL_BLOCK - 1)).astype(jnp.float32)
    ks_blk = kv_t(ks).reshape(B, G, n_sel, NSA_SEL_BLOCK, dh)
    vs_blk = kv_t(vs).reshape(B, G, n_sel, NSA_SEL_BLOCK, dh)
    pad = ((0, 0), (0, 0), (NSA_WINDOW, 0), (0, 0))
    kw_pad = jnp.pad(kv_t(kw), pad)
    vw_pad = jnp.pad(kv_t(vw), pad)

    tbl = bias_tbl.T.reshape(G, Hg, REL_BUCKETS)
    win_len = NSA_WINDOW + Q_BLOCK
    rel = jnp.arange(Q_BLOCK)[:, None] + NSA_WINDOW - jnp.arange(win_len)[None, :]
    win_bias = tbl[:, :, t5_bucket(rel)]
    win_rel_mask = (rel >= 0) & (rel < NSA_WINDOW)
    top_n = min(NSA_SEL_TOPN, n_sel)
    b_ix = jnp.arange(B)[:, None, None, None]
    g_ix = jnp.arange(G)[None, :, None, None]
    g_ix5 = jnp.arange(G)[None, :, None, None, None]
    h_ix5 = jnp.arange(Hg)[None, None, :, None, None]
    blk = jnp.arange(n_sel)

    def block(i):
        s0 = i * Q_BLOCK
        t = s0 + jnp.arange(Q_BLOCK)
        qb = lax.dynamic_slice_in_dim(qh, s0, Q_BLOCK, axis=3)
        gb = lax.dynamic_slice_in_dim(gh, s0, Q_BLOCK, axis=3)
        sc = jnp.einsum('bghqd,bgcd->bghqc', qb, k_cmp) * scale
        pc = masked_softmax(sc, cmp_end[None, :] <= t[:, None])
        o_cmp = jnp.einsum('bghqc,bgcd->bghqd', pc.astype(v_cmp.dtype), v_cmp)
        imp = jnp.einsum('bghqc,cn->bgqn', pc, overlap)
        cur = t // NSA_SEL_BLOCK
        forced = (blk[None, :] == 0) | (blk[None, :] == cur[:, None]) | (blk[None, :] == cur[:, None] - 1)
        valid = blk[None, :] <= cur[:, None]
        imp = jnp.where(forced, NSA_FORCE_SCORE, jnp.where(valid, imp, -1.0))
        _, sel = lax.top_k(imp, top_n)
        k_sel = ks_blk[b_ix, g_ix, sel].reshape(B, G, Q_BLOCK, top_n * NSA_SEL_BLOCK, dh)
        v_sel = vs_blk[b_ix, g_ix, sel].reshape(B, G, Q_BLOCK, top_n * NSA_SEL_BLOCK, dh)
        pos = (sel[..., None] * NSA_SEL_BLOCK + jnp.arange(NSA_SEL_BLOCK)).reshape(B, G, Q_BLOCK, top_n * NSA_SEL_BLOCK)
        dist = t[:, None] - pos
        bias = tbl[g_ix5, h_ix5, t5_bucket(dist)[:, :, None]]
        ss = jnp.einsum('bghqd,bgqkd->bghqk', qb, k_sel) * scale + bias
        ps = masked_softmax(ss, (dist >= 0)[:, :, None])
        o_sel = jnp.einsum('bghqk,bgqkd->bghqd', ps.astype(v_sel.dtype), v_sel)
        k_win = lax.dynamic_slice_in_dim(kw_pad, s0, win_len, axis=2)
        v_win = lax.dynamic_slice_in_dim(vw_pad, s0, win_len, axis=2)
        kpos = s0 - NSA_WINDOW + jnp.arange(win_len)
        sw = jnp.einsum('bghqd,bgkd->bghqk', qb, k_win) * scale + win_bias
        pw = masked_softmax(sw, win_rel_mask & (kpos >= 0)[None, :])
        o_win = jnp.einsum('bghqk,bgkd->bghqd', pw.astype(v_win.dtype), v_win)
        return gb[..., 0:1] * o_cmp + gb[..., 1:2] * o_sel + gb[..., 2:3] * o_win

    out = lax.map(block, jnp.arange(S // Q_BLOCK))
    return out.transpose(1, 0, 4, 2, 3, 5).reshape(B, S, G * Hg * dh)

def swa_sink_mixer(q, k, v, sinks, bias_tbl):
    B, S, _ = q.shape
    G, Hg, dh = SWA_KV_HEADS, SWA_Q_HEADS // SWA_KV_HEADS, HEAD_DIM
    scale = dh ** -0.5
    qh = q.reshape(B, S, G, Hg, dh).transpose(0, 2, 3, 1, 4)
    pad = ((0, 0), (0, 0), (SWA_WINDOW, 0), (0, 0))
    k_pad = jnp.pad(k.reshape(B, S, G, dh).transpose(0, 2, 1, 3), pad)
    v_pad = jnp.pad(v.reshape(B, S, G, dh).transpose(0, 2, 1, 3), pad)
    win_len = SWA_WINDOW + Q_BLOCK
    rel = jnp.arange(Q_BLOCK)[:, None] + SWA_WINDOW - jnp.arange(win_len)[None, :]
    bias = bias_tbl.T.reshape(G, Hg, REL_BUCKETS)[:, :, t5_bucket(rel)]
    rel_mask = (rel >= 0) & (rel < SWA_WINDOW)
    sink = sinks.reshape(G, Hg)

    def block(i):
        s0 = i * Q_BLOCK
        qb = lax.dynamic_slice_in_dim(qh, s0, Q_BLOCK, axis=3)
        kb = lax.dynamic_slice_in_dim(k_pad, s0, win_len, axis=2)
        vb = lax.dynamic_slice_in_dim(v_pad, s0, win_len, axis=2)
        kpos = s0 - SWA_WINDOW + jnp.arange(win_len)
        s = jnp.einsum('bghqd,bgkd->bghqk', qb, kb) * scale + bias
        p = sink_softmax(s, rel_mask & (kpos >= 0)[None, :], sink)
        return jnp.einsum('bghqk,bgkd->bghqd', p.astype(vb.dtype), vb)

    out = lax.map(block, jnp.arange(S // Q_BLOCK))
    return out.transpose(1, 0, 4, 2, 3, 5).reshape(B, S, G * Hg * dh)

def peer_ffn(z, wq, subkeys, u_tab, v_tab):
    B, S, D = z.shape
    Hp, K, half = PEER_HEADS, PEER_TOPK, PEER_QDIM // 2
    zt = z.reshape(B * S // PEER_TOK_BLOCK, PEER_TOK_BLOCK, D)

    def block(zb):
        q = (zb @ wq).reshape(PEER_TOK_BLOCK, Hp, 2, half)
        s = jnp.einsum('thpd,hpnd->thpn', q, subkeys).astype(jnp.float32)
        s_top, i_top = lax.top_k(s, K)
        cand = (s_top[:, :, 0, :, None] + s_top[:, :, 1, None, :]).reshape(PEER_TOK_BLOCK, Hp, K * K)
        score, flat = lax.top_k(cand, K)
        i1 = jnp.take_along_axis(i_top[:, :, 0], flat // K, axis=-1)
        i2 = jnp.take_along_axis(i_top[:, :, 1], flat % K, axis=-1)
        expert = i1 * PEER_NKEYS + i2
        gate = jax.nn.softmax(score, axis=-1)
        h = jnp.einsum('thkd,td->thk', u_tab[expert], zb).astype(jnp.float32)
        act = (gate * jax.nn.gelu(h, approximate=False)).astype(zb.dtype)
        return jnp.einsum('thk,thkd->td', act, v_tab[expert])

    return lax.map(block, zt).reshape(B, S, D)

def second_inputs(seed: int = 0) -> dict:
    key = jax.random.key(seed)
    keys = iter(jax.random.split(key, 40))
    L, D = DEPTH, D_MODEL

    def nrm(shape, scale):
        return jax.random.normal(next(keys), shape, jnp.float32) * scale

    def unif(shape, lo, hi):
        return jax.random.uniform(next(keys), shape, jnp.float32, lo, hi)

    cmp_in = NSA_CMP_LEN * HEAD_DIM
    return {
        'x': nrm((BATCH, SEQ, D), 1.0),
        'ln1_w': 1.0 + nrm((L, D), 0.02),
        'ln2_w': 1.0 + nrm((L, D), 0.02),
        'lnf_w': 1.0 + nrm((D,), 0.02),
        'rel_bias': nrm((REL_BUCKETS, NSA_Q_HEADS + SWA_Q_HEADS), 0.3),
        'w_in': nrm((L, D, IN_COLS), D ** -0.5),
        'rwkv_mu': unif((L, RWKV_COLS), 0.0, 1.0),
        'rwkv_w0': -0.5 + nrm((L, RWKV_WIDTH), 0.5),
        'rwkv_w2': nrm((L, RWKV_DECAY_RANK, RWKV_WIDTH), 0.1),
        'rwkv_a0': nrm((L, RWKV_WIDTH), 0.3),
        'rwkv_a2': nrm((L, RWKV_ICLR_RANK, RWKV_WIDTH), 0.1),
        'rwkv_g2': nrm((L, RWKV_GATE_RANK, RWKV_WIDTH), RWKV_GATE_RANK ** -0.5),
        'rwkv_k_k': 0.85 + nrm((L, RWKV_WIDTH), 0.05),
        'rwkv_k_a': 1.0 + nrm((L, RWKV_WIDTH), 0.05),
        'rwkv_r_k': nrm((L, RWKV_HEADS, HEAD_DIM), 0.1),
        'rwkv_ln_w': 1.0 + nrm((L, RWKV_WIDTH), 0.02),
        'rwkv_ln_b': nrm((L, RWKV_WIDTH), 0.02),
        'nsa_pe_k': nrm((L, NSA_CMP_LEN, HEAD_DIM), 0.1),
        'nsa_pe_v': nrm((L, NSA_CMP_LEN, HEAD_DIM), 0.1),
        'nsa_ck_w1': nrm((L, cmp_in, NSA_CMP_HIDDEN), cmp_in ** -0.5),
        'nsa_ck_w2': nrm((L, NSA_CMP_HIDDEN, HEAD_DIM), NSA_CMP_HIDDEN ** -0.5),
        'nsa_cv_w1': nrm((L, cmp_in, NSA_CMP_HIDDEN), cmp_in ** -0.5),
        'nsa_cv_w2': nrm((L, NSA_CMP_HIDDEN, HEAD_DIM), NSA_CMP_HIDDEN ** -0.5),
        'swa_sinks': nrm((L, SWA_Q_HEADS), 0.5),
        'w_br_a': nrm((L, RWKV_WIDTH, D), RWKV_WIDTH ** -0.5),
        'w_br_b': nrm((L, NSA_Q_HEADS * HEAD_DIM, D), (NSA_Q_HEADS * HEAD_DIM) ** -0.5),
        'w_br_c': nrm((L, SWA_Q_HEADS * HEAD_DIM, D), (SWA_Q_HEADS * HEAD_DIM) ** -0.5),
        'w_out': nrm((L, D, D), D ** -0.5),
        'peer_wq': nrm((L, D, PEER_HEADS * PEER_QDIM), D ** -0.5),
        'peer_subkeys': nrm((L, PEER_HEADS, 2, PEER_NKEYS, PEER_QDIM // 2), (PEER_QDIM // 2) ** -0.5),
        'peer_u': nrm((L, PEER_EXPERTS, D), D ** -0.5),
        'peer_v': nrm((L, PEER_EXPERTS, D), 0.5 * PEER_HEADS ** -0.5),
    }

def second_block(x, ln1_w, ln2_w, lnf_w, rel_bias, w_in, rwkv_mu, rwkv_w0, rwkv_w2, rwkv_a0, rwkv_a2,
              rwkv_g2, rwkv_k_k, rwkv_k_a, rwkv_r_k, rwkv_ln_w, rwkv_ln_b, nsa_pe_k, nsa_pe_v,
              nsa_ck_w1, nsa_ck_w2, nsa_cv_w1, nsa_cv_w2, swa_sinks, w_br_a, w_br_b, w_br_c, w_out,
              peer_wq, peer_subkeys, peer_u, peer_v):
    nsa_tbl = rel_bias[:, :NSA_Q_HEADS]
    swa_tbl = rel_bias[:, NSA_Q_HEADS:]
    for l in range(DEPTH):
        u = rmsnorm(x, ln1_w[l])
        proj = u @ w_in[l]
        rw = token_shift(proj[..., :RWKV_COLS], rwkv_mu[l])
        zr, zk, zv, zw, za, zg = split_cols(rw, RWKV_SPLITS)
        cols = split_cols(proj[..., RWKV_COLS:], NSA_SPLITS + SWA_SPLITS + GATE_SPLITS)
        nq, nkc, nvc, nks, nvs, nkw, nvw, ngate = cols[:8]
        sq, sk, sv = cols[8:11]
        g_a, g_b, g_c = [jax.nn.sigmoid(c) for c in cols[11:14]]
        o_a = rwkv7_mixer(zr, zk, zv, zw, za, zg, rwkv_w0[l], rwkv_w2[l], rwkv_a0[l], rwkv_a2[l],
                          rwkv_g2[l], rwkv_k_k[l], rwkv_k_a[l], rwkv_r_k[l], rwkv_ln_w[l], rwkv_ln_b[l])
        o_b = nsa_mixer(nq, nkc, nvc, nks, nvs, nkw, nvw, ngate, nsa_pe_k[l], nsa_pe_v[l],
                        nsa_ck_w1[l], nsa_ck_w2[l], nsa_cv_w1[l], nsa_cv_w2[l], nsa_tbl)
        o_c = swa_sink_mixer(sq, sk, sv, swa_sinks[l], swa_tbl)
        merged = g_a * (o_a @ w_br_a[l]) + g_b * (o_b @ w_br_b[l]) + g_c * (o_c @ w_br_c[l])
        x = x + merged @ w_out[l]
        x = x + peer_ffn(rmsnorm(x, ln2_w[l]), peer_wq[l], peer_subkeys[l], peer_u[l], peer_v[l])
    return rmsnorm(x, lnf_w)


def setup_inputs(seed=0):
    out = dict(first_inputs(seed))
    for name, value in second_inputs(seed + 1).items():
        if name != "x":
            out[name + "_2"] = value
    return out


def reference(
    x, c, ctx, c_ctx, w_ada, b_ada, norm1_w, norm2_w, w_in, lam_qk, subln_w, lb_param,
    hgrn_norm_w, w_fnet, w_out, w_up, conv_w, conv_b, w_down, final_norm_w, ln1_w_2, ln2_w_2,
    lnf_w_2, rel_bias_2, w_in_2, rwkv_mu_2, rwkv_w0_2, rwkv_w2_2, rwkv_a0_2, rwkv_a2_2,
    rwkv_g2_2, rwkv_k_k_2, rwkv_k_a_2, rwkv_r_k_2, rwkv_ln_w_2, rwkv_ln_b_2, nsa_pe_k_2,
    nsa_pe_v_2, nsa_ck_w1_2, nsa_ck_w2_2, nsa_cv_w1_2, nsa_cv_w2_2, swa_sinks_2, w_br_a_2,
    w_br_b_2, w_br_c_2, w_out_2, peer_wq_2, peer_subkeys_2, peer_u_2, peer_v_2,
):
    x = first_block(
        x, c, ctx, c_ctx, w_ada, b_ada, norm1_w, norm2_w, w_in, lam_qk, subln_w, lb_param,
        hgrn_norm_w, w_fnet, w_out, w_up, conv_w, conv_b, w_down, final_norm_w,
    )
    return second_block(
        x, ln1_w_2, ln2_w_2, lnf_w_2, rel_bias_2, w_in_2, rwkv_mu_2, rwkv_w0_2, rwkv_w2_2,
        rwkv_a0_2, rwkv_a2_2, rwkv_g2_2, rwkv_k_k_2, rwkv_k_a_2, rwkv_r_k_2, rwkv_ln_w_2,
        rwkv_ln_b_2, nsa_pe_k_2, nsa_pe_v_2, nsa_ck_w1_2, nsa_ck_w2_2, nsa_cv_w1_2, nsa_cv_w2_2,
        swa_sinks_2, w_br_a_2, w_br_b_2, w_br_c_2, w_out_2, peer_wq_2, peer_subkeys_2, peer_u_2,
        peer_v_2,
    )


_drawn_inputs = setup_inputs


def setup_inputs(seed=0):
    import zlib

    import numpy as np

    out = dict(_drawn_inputs(seed))
    spreads = {}
    factors = {'lam_qk': 3.013,
     'hgrn_norm_w': 3.938,
     'conv_b': 3.164,
     'ln2_w_2': 3.165,
     'lnf_w_2': 2.843,
     'rwkv_k_k_2': 4.699,
     'rwkv_ln_w_2': 4.182,
     'rwkv_ln_b_2': 3.779,
     'nsa_pe_k_2': 6.508,
     'swa_sinks_2': 5.327}
    for name, (base, spread) in spreads.items():
        noise = np.random.default_rng([zlib.crc32(name.encode()), seed]).standard_normal(out[name].shape)
        drawn = base * np.exp(spread * noise) if base else spread * noise
        out[name] = __import__('jax').numpy.asarray(drawn.astype(out[name].dtype))
    for name, factor in factors.items():
        out[name] = (out[name] * factor).astype(out[name].dtype)
    return out
```

```python
import math
from contextlib import ExitStack

import numpy as np

import concourse.bass as bass
from concourse import mybir

F32 = mybir.dt.float32
U32 = mybir.dt.uint32
ALU = mybir.AluOpType
ACT = mybir.ActivationFunctionType
AX = mybir.AxisListType.X

P = 128
D = 1024
DC = D // P
SEQ = 256
CTX = 256
TOK = CTX + SEQ
DEPTH = 2
EPS = 1e-6
HA, DHA, DVA = 4, 64, 128
DFF = 2816
FC = DFF // P
PROJ1 = 3072
NEG = -1.0e30
PANEL = 256
RING = 5
ROWS = 6
BANKS = 4

QA, KA, VA, QH, ZF, ZB, IH, GH, UF = 0, 4, 8, 12, 14, 16, 18, 20, 22
ZR, ZK, ZV, ZWA, ZG, NQ, KC, VC, KS, VS, KW, VW, SQ, SK, SV, GATES, NG = (
    0, 4, 8, 12, 13, 14, 18, 19, 20, 21, 22, 23, 24, 28, 29, 30, 54)
IN_A, IN_G = 3072, 24
RH, NSA_H, HKP = 8, 8, 16
TOPK = 16
PEER_H = 8
NKEYS = 128


def table_layout(entries):
    at, out = 0, {}
    for name, width in entries:
        out[name] = (at, width)
        at += width
    return out, at


T1, T1_W = table_layout([
    ("ident", 128), ("ones", 128), ("block", 128), ("rot", 128), ("cos", 256), ("sin", 256),
    ("dftd", 256), ("dftt", 1024)])
T2, T2_W = table_layout([
    ("ident", 128), ("ones", 128), ("block", 128), ("flip", 128),
    ("low16", 128), ("up16", 128), ("low32", 128), ("low64", 128), ("low128", 128),
    ("upper", 128), ("upper_inc", 128), ("dup", 512), ("half", 2), ("bucket_full", 384),
    ("bucket_win", 384), ("cmp_mask", 32), ("iota16", 16)])


def t5_bucket_np(n, buckets=32, max_dist=128):
    exact = buckets // 2
    nf = np.maximum(n, exact).astype(np.float32)
    large = exact + (np.log(nf / np.float32(exact)) / np.float32(math.log(max_dist / exact))
                     * np.float32(buckets - exact)).astype(np.int32)
    return np.where(n < exact, n, np.minimum(large, buckets - 1))


def constant_tables():
    i = np.arange(P)
    ident = np.eye(P, dtype=np.float32)
    ones = np.ones((P, P), np.float32)
    block = (i[:, None] // 64 == i[None, :] // 64).astype(np.float32)
    rot = np.zeros((P, P), np.float32)
    for m in range(P):
        if m % 32 < 16:
            rot[m + 16, m] = -1.0
        else:
            rot[m - 16, m] = 1.0
    t = np.arange(SEQ)
    half = DHA // 2
    inv = (np.float32(10000.0) ** (-np.arange(0, half, 2, dtype=np.float32) / half)).astype(np.float32)
    ar = (t // 64).astype(np.float32)[:, None] * inv
    ac = (t % 64).astype(np.float32)[:, None] * inv
    ang = np.concatenate([ar, ar, ac, ac], -1).astype(np.float32)
    cos = np.tile(np.cos(ang).T, (2, 1))
    sin = np.tile(np.sin(ang).T, (2, 1))
    d = np.arange(64)
    phase = 2 * np.pi * ((d[:, None] * d[None, :]) % 64) / 64
    dftd = np.concatenate([np.kron(np.eye(2), np.cos(phase)), np.kron(np.eye(2), np.sin(phase))], 1)
    phase = 2 * np.pi * ((t[:, None] * t[None, :]) % SEQ) / SEQ
    scale = 1.0 / math.sqrt(SEQ * 64)
    ct, st = np.cos(phase) * scale, -np.sin(phase) * scale
    dftt = np.concatenate([ct[0:P], st[0:P], ct[P:], st[P:]], 1)
    one = dict(ident=ident, ones=ones, block=block, rot=rot, cos=cos, sin=sin, dftd=dftd,
               dftt=dftt)
    r, c = i[:, None], i[None, :]
    low = r > c

    def level(n):
        return (r // n == c // n) & (r // (n // 2) > c // (n // 2))

    dup = np.zeros((P, 4, P), np.float32)
    for g in range(2):
        for hh in range(2):
            for j in range(64):
                dup[g * 64 + j, g * 2 + hh, hh * 64 + j] = 1.0
    m = np.arange(384)
    dist = 255 - m
    full = np.zeros((P, 384), np.float32)
    win = np.zeros((P, 384), np.float32)
    for x in range(384):
        ok = dist[x] >= 0
        full[t5_bucket_np(max(dist[x], 0)) if ok else 32, x] = 1.0
        win[t5_bucket_np(max(dist[x], 0)) if ok and dist[x] < 128 else 32, x] = 1.0
    cmask = np.zeros((P, 2, 16), np.float32)
    for q in range(2):
        cmask[:, q, :] = (np.arange(16)[None] * 16 + 31 <= (q * P + i)[:, None])
    cmask[:, :, 15] = 0.0
    halves = np.stack([(i < 64), (i >= 64)], 1)
    two = dict(ident=ident, ones=ones, block=block, flip=ident[::-1],
               low16=low & (r // 16 == c // 16), up16=(r < c) & (r // 16 == c // 16),
               low32=level(32), low64=level(64), low128=level(128),
               upper=r < c, upper_inc=r <= c, dup=dup.reshape(P, 512), half=halves,
               bucket_full=full, bucket_win=win, cmp_mask=cmask.reshape(P, 32),
               iota16=np.tile(np.arange(16), (P, 1)))
    pack = lambda lay, arrs: np.concatenate([np.asarray(arrs[n], np.float32) for n in lay], 1)
    return np.ascontiguousarray(pack(T1, one)), np.ascontiguousarray(pack(T2, two))


def recurrence_masks():
    s, t = np.arange(P)[:, None], np.arange(P)[None, :]
    out = np.zeros((P, 2, 7, P), np.float32)
    for i in range(7):
        size = 2 << i
        same, left_s, left_t = s // size == t // size, s % size < size // 2, t % size < size // 2
        out[:, 0, i] = same & left_s & ~left_t
        out[:, 1, i] = same & ~left_s & left_t
    return np.ascontiguousarray(out.reshape(P, -1))


V1, _ = table_layout([("norm1", 8), ("norm2", 8), ("subln", 1), ("hnorm", 1), ("lb", 8), ("b_ada", 48),
                      ("cond", 16), ("final", 8)])
V2, _ = table_layout([("ln1", 8), ("ln2", 8), ("mu", 14), ("w0", 4), ("a0", 4), ("kk", 4), ("ka", 4),
                      ("rk", 4), ("lnw", 4), ("lnb", 4), ("lnf", 8)])
PACK1 = [0, 128]
PACKC = [(256, 384), (512, 640)]
PACK2 = [768, 896]
VEC_W = 1024


class Counts(dict):

    def __missing__(self, name):
        return 0

    def next(self, name, by=1):
        self[name] = self[name] + by
        return self[name]


def weight_panels(a):
    out = []

    def add(w, cols0, cols, r0=0, rows=None):
        rows = w.shape[0] if rows is None else rows
        out.append(("matrix", w[r0:r0 + rows, cols0:cols0 + cols], rows, cols))

    for j in range(24):
        add(a["w_ada"][0], j * PANEL, PANEL)
    for l in range(DEPTH):
        for j in range(12):
            add(a["w_in"][l], j * PANEL, PANEL)
        add(a["w_fnet"][l], 0, PANEL)
        if l < DEPTH - 1:
            for j in range(24):
                add(a["w_ada"][l + 1], j * PANEL, PANEL)
        for j in range(4):
            add(a["w_out"][l], j * PANEL, PANEL)
        for j in range(11):
            add(a["w_up"][l], j * PANEL, PANEL)
            add(a["w_up"][l], DFF + j * PANEL, PANEL)
        for j in range(4):
            for r0, rows in ((0, 1024), (1024, 1024), (2048, 768)):
                add(a["w_down"][l], j * PANEL, PANEL, r0, rows)
    for l in range(DEPTH):
        for j in range(12):
            add(a["w_in_2"][l], j * PANEL, PANEL)
        add(a["w_in_2"][l], IN_A, IN_G)
        for j in range(11):
            add(a["w_in_2"][l], IN_A + IN_G + j * PANEL, PANEL)
        for w in (a["nsa_ck_w1_2"][l], a["nsa_cv_w1_2"][l]):
            for half in range(4):
                out.append(("cmp", w, half))
        for j in range(4):
            add(a["w_in_2"][l], IN_A + IN_G + (11 + j) * PANEL, PANEL)
            add(a["w_br_a_2"][l], j * PANEL, PANEL)
        for w in (a["w_br_b_2"][l], a["w_br_c_2"][l]):
            for j in range(4):
                add(w, j * PANEL, PANEL)
        for j in range(4):
            add(a["w_out_2"][l], j * PANEL, PANEL)
        out.append(("subkeys", a["peer_subkeys_2"][l]))
        for j in range(8):
            add(a["peer_wq_2"][l], j * PANEL, PANEL)
    return out


def panel_values(a):
    value, out = [0] * RING, []
    for i, panel in enumerate(weight_panels(a)):
        value[i % RING] += 32 if panel[0] == "cmp" else 16
        out.append(value[i % RING])
    return out


def load_panels(sp, cnt, sem, k):
    for i, panel in enumerate(k.panels):
        slot = k.ring[:, (i % RING) * 2048:(i % RING + 1) * 2048]
        if i >= RING:
            sp.wait_ge(sem.panel_used, i - RING + 2)
        if panel[0] == "cmp":
            src = panel[1].rearrange("(l d) n -> d l n", d=64)[:, panel[2] * 8:panel[2] * 8 + 8, :]
            dst = slot.rearrange("p (l n) -> p l n", l=8)
            sp.dma_start(dst[0:64], src).then_inc(sem.panel_loaded[i % RING], 16)
            sp.dma_start(dst[64:128], src).then_inc(sem.panel_loaded[i % RING], 16)
        elif panel[0] == "subkeys":
            sp.dma_start(slot.rearrange("p (h d) -> p h d", d=128),
                         panel[1].rearrange("h t n d -> n (h t) d")).then_inc(sem.panel_loaded[i % RING], 16)
        else:
            _, src, rows, cols = panel
            kc = rows // P
            sp.dma_start(slot[:, 0:kc * cols].rearrange("p (c n) -> p c n", c=kc),
                         src.rearrange("(c p) n -> p c n", p=P)).then_inc(sem.panel_loaded[i % RING], 16)


def vectors_to_columns_tensor(pe, cnt, sem, k, packs):
    for c0, _ in packs:
        pe.wait_ge(sem.act_bank_free, cnt["act_bank"] + 1)
        bank = k.bank["act"][cnt["act_bank"] % BANKS]
        pe.transpose(bank[:, 0:P], k.rows[:, c0:c0 + P], k.ident).then_inc(sem.act_bank_filled, 1)
        cnt.next("act_bank")


def vectors_to_columns_scalar(act, cnt, sem, k, packs):
    for c0, _ in packs:
        act.wait_ge(sem.act_bank_filled, cnt.next("act_bank"))
        bank = k.bank["act"][(cnt["act_bank"] - 1) % BANKS]
        act.activation(k.vec[:, c0:c0 + P], bank[:, 0:P], ACT.Copy).then_inc(sem.act_bank_free, 1)


def tokens_to_features_tensor(pe, cnt, sem, k, src, tiles):
    for c in range(DC):
        for t0 in range(0, tiles, 4):
            pe.wait_ge(sem.act_bank_free, cnt["act_bank"] + 1)
            bank = k.bank["act"][cnt["act_bank"] % BANKS]
            n = min(4, tiles - t0)
            for t in range(n):
                ins = pe.transpose(bank[:, t * P:(t + 1) * P], src[:, t0 + t, c * P:(c + 1) * P], k.ident)
            ins.then_inc(sem.act_bank_filled, 1)
            cnt.next("act_bank")


def norm_vector(dve, cnt, sem, k, src, tok, dst=None):
    dst = k.xn if dst is None else dst
    n = tok[1] - tok[0]
    x, y = src[:, :, tok[0]:tok[1]], dst[:, :, tok[0]:tok[1]]
    for c in range(DC):
        dve.tensor_tensor(y[:, c, :], x[:, c, :], x[:, c, :], ALU.mult).then_inc(sem.square_chunk_ready, 1)
    dve.wait_ge(sem.dve_bank_filled, cnt.next("dve_bank"))
    bank = k.bank["dve"][(cnt["dve_bank"] - 1) % BANKS]
    dve.tensor_scalar(k.rms[:, 0:n], bank[:, 0:n], 1.0 / D, EPS, ALU.mult, ALU.add).then_inc(sem.dve_bank_free, 1)
    dve.wait_ge(sem.dve_bank_free, BANKS + cnt["dve_bank"])
    dve.nop().then_inc(sem.mean_square_ready, 1)
    cnt.next("mean_square_ready given")
    dve.wait_ge(sem.root_ready, cnt.next("root_ready"))
    dve.reciprocal(k.rms[:, 0:n], k.rms[:, 0:n]).then_inc(sem.dve_done, 1)
    dve.wait_ge(sem.dve_done, cnt.next("dve_done"))


def norm_tensor(pe, cnt, sem, k, tok, dst=None):
    dst = k.xn if dst is None else dst
    n = tok[1] - tok[0]
    pe.wait_ge(sem.dve_bank_free, cnt["dve_bank"] + 1)
    bank = k.bank["dve"][cnt["dve_bank"] % BANKS]
    for c in range(DC):
        pe.wait_ge(sem.square_chunk_ready, cnt.next("square_chunk_ready"))
        ins = pe.matmul(bank[:, 0:n], k.ones, dst[:, c, tok[0]:tok[1]],
                          start=(c == 0), stop=(c == DC - 1))
    ins.then_inc(sem.dve_bank_filled, 1)
    cnt.next("dve_bank")


def root_scalar(act, cnt, sem, k, ap):
    act.wait_ge(sem.mean_square_ready, cnt.next("mean_square_ready"))
    act.activation(ap, ap, ACT.Sqrt).then_inc(sem.root_ready, 1)
    act.wait_ge(sem.root_ready, cnt.next("root_ready given"))


def group_norm_vector(dve, cnt, sem, k, x, sq, chunks, n, width, eps, clamp=None):
    dve.tensor_tensor(sq, x, x, ALU.mult).then_inc(sem.squares_ready, 1)
    dve.wait_ge(sem.squares_ready, cnt.next("squares_ready given"))
    for c in range(chunks):
        dve.wait_ge(sem.dve_bank_filled, cnt.next("dve_bank"))
        bank = k.bank["dve"][(cnt["dve_bank"] - 1) % BANKS]
        if clamp is None:
            ins = dve.tensor_scalar(sq[:, c, :], bank[:, 0:n], 1.0 / width, eps, ALU.mult, ALU.add)
        else:
            ins = dve.tensor_scalar(sq[:, c, :], bank[:, 0:n], clamp, None, ALU.max)
        ins.then_inc(sem.dve_bank_free, 1)
    dve.wait_ge(sem.dve_bank_free, BANKS + cnt["dve_bank"])
    dve.nop().then_inc(sem.mean_square_ready, 1)
    cnt.next("mean_square_ready given")
    dve.wait_ge(sem.root_ready, cnt.next("root_ready"))
    dve.reciprocal(sq, sq).then_inc(sem.dve_done, 1)
    dve.wait_ge(sem.dve_done, cnt.next("dve_done"))
    dve.tensor_tensor(x, x, sq, ALU.mult).then_inc(sem.dve_done, 1)
    dve.wait_ge(sem.dve_done, cnt.next("dve_done"))


def group_norm_tensor(pe, cnt, sem, k, sq, chunks, n, ones):
    pe.wait_ge(sem.squares_ready, cnt.next("squares_ready"))
    for c in range(chunks):
        pe.wait_ge(sem.dve_bank_free, cnt["dve_bank"] + 1)
        bank = k.bank["dve"][cnt["dve_bank"] % BANKS]
        pe.matmul(bank[:, 0:n], ones, sq[:, c, :], start=True, stop=True).then_inc(sem.dve_bank_filled, 1)
        cnt.next("dve_bank")


LAYER1_FULL = set(range(KA, QH)) | set(range(ZF, GH))


def tokens_of(l, chunk=None):
    if l < DEPTH - 1 or (chunk is not None and chunk in LAYER1_FULL):
        return 0
    return CTX


def cond_stage_scalar(act, cnt, sem, k):
    act.wait_ge(sem.act_bank_free, BANKS + cnt["act_bank"])
    act.activation(k.cond[:, :, :], k.v1(0, "cond").rearrange("p (s c) -> p c s", s=2), ACT.Silu).then_inc(sem.cond_ready, 1)
    act.wait_ge(sem.cond_ready, cnt.next("cond_ready given"))


ADA_STEPS = 6 * D // PANEL + 1


def ada_tensor(pe, cnt, sem, k, steps):
    for j in range(steps[0], steps[1]):
        if j < ADA_STEPS - 1:
            pe.wait_ge(sem.panel_loaded[cnt["panel"] % RING], k.panel_value[cnt["panel"]])
            panel = k.panel(cnt.next("panel") - 1)
            pe.wait_ge(sem.act_bank_free, cnt["act_bank"] + 1)
            bank = k.bank["act"][cnt["act_bank"] % BANKS]
            for kc in range(DC):
                ins = pe.matmul(bank[0:2, 0:PANEL], k.cond[:, kc, :], panel[:, kc, :],
                                  start=(kc == 0), stop=(kc == DC - 1))
                if kc == 0:
                    ins.then_inc(sem.panel_used, 1)
            ins.then_inc(sem.act_bank_filled, 1)
            cnt.next("act_bank")
            row_banks = cnt["act_bank"]
        if j > 0:
            pe.wait_ge(sem.act_bank_free, BANKS + cnt["ada_row_bank"])
            pe.wait_ge(sem.act_bank_free, cnt["act_bank"] + 1)
            bank = k.bank["act"][cnt["act_bank"] % BANKS]
            for m in range(2):
                ins = pe.transpose(bank[:, 2 * m:2 * m + 2], k.adarow[0:2, (j - 1) % 2, m * P:(m + 1) * P],
                                     k.ident[0:2, 0:2])
            ins.then_inc(sem.act_bank_filled, 1)
            cnt.next("act_bank")
        if j < ADA_STEPS - 1:
            cnt["ada_row_bank"] = row_banks


def ada_scalar(act, cnt, sem, k, steps):
    for j in range(steps[0], steps[1]):
        if j < ADA_STEPS - 1:
            act.wait_ge(sem.act_bank_filled, cnt.next("act_bank"))
            bank = k.bank["act"][(cnt["act_bank"] - 1) % BANKS]
            act.activation(k.adarow[0:2, j % 2, :], bank[0:2, 0:PANEL], ACT.Copy).then_inc(sem.act_bank_free, 1)
        if j > 0:
            act.wait_ge(sem.act_bank_filled, cnt.next("act_bank"))
            bank = k.bank["act"][(cnt["act_bank"] - 1) % BANKS]
            act.activation(k.modraw[:, 2 * j - 2:2 * j, :],
                                                bank[:, 0:4].rearrange("p (m s) -> p m s", m=2), ACT.Copy).then_inc(sem.act_bank_free, 1)
    if steps[1] == ADA_STEPS:
        act.wait_ge(sem.act_bank_free, BANKS + cnt["act_bank"])
        act.nop().then_inc(sem.ada_ready, 1)
        cnt.next("ada_ready given")


def ada_vector(dve, cnt, sem, k, l):
    dve.wait_ge(sem.ada_ready, cnt.next("ada_ready"))
    dve.tensor_tensor(k.mod[:, :, :], k.modraw[:, :, :],
                               k.v1(l, "b_ada").unsqueeze(2).to_broadcast([P, 48, 2]), ALU.add).then_inc(sem.dve_done, 1)
    dve.wait_ge(sem.dve_done, cnt.next("dve_done"))
    for which, (sc, norm) in enumerate(((8, "norm1"), (32, "norm2"))):
        dve.tensor_scalar(k.modw[:, which, :, :], k.mod[:, sc:sc + 8, :], 1.0, None, ALU.add).then_inc(sem.dve_done, 1)
        dve.wait_ge(sem.dve_done, cnt.next("dve_done"))
        dve.tensor_tensor(k.modw[:, which, :, :], k.modw[:, which, :, :],
                                   k.v1(l, norm).unsqueeze(2).to_broadcast([P, 8, 2]), ALU.mult).then_inc(sem.dve_done, 1)
        dve.wait_ge(sem.dve_done, cnt.next("dve_done"))


def normalise_vector(dve, cnt, sem, k, tok):
    n = tok[1] - tok[0]
    for c in range(DC):
        dve.tensor_tensor(k.xn[:, c, tok[0]:tok[1]], k.x[:, c, tok[0]:tok[1]], k.rms[:, 0:n], ALU.mult
                            ).then_inc(sem.normalised_chunk_ready, 1)


def modulate_scalar(act, cnt, sem, k, which, t0):
    shift = 0 if which == 0 else 24
    for c in range(DC):
        act.wait_ge(sem.normalised_chunk_ready, cnt.next("normalised_chunk_ready"))
        for s in range(t0 // CTX, 2):
            a, b = s * CTX, s * CTX + SEQ
            ins = act.activation(k.xn[:, c, a:b], k.xn[:, c, a:b], ACT.Identity, bias=k.mod[:, shift + c, s:s + 1],
                                   scale=k.modw[:, which, c, s:s + 1])
        ins.then_inc(sem.xn_ready, 1)


def project_tensor(pe, cnt, sem, k, l):
    for j in range(PROJ1 // PANEL):
        pe.wait_ge(sem.panel_loaded[cnt["panel"] % RING], k.panel_value[cnt["panel"]])
        panel = k.panel(cnt.next("panel") - 1)
        for m in range(2):
            t0 = tokens_of(l, 2 * j + m)
            pe.wait_ge(sem.act_bank_free, cnt["act_bank"] + 1)
            bank = k.bank["act"][cnt["act_bank"] % BANKS]
            for kc in range(DC):
                if j == 0 and m == 0:
                    pe.wait_ge(sem.xn_ready, cnt.next("xn_ready"))
                ins = pe.matmul(bank[:, t0:TOK], panel[:, kc, m * P:(m + 1) * P], k.xn[:, kc, t0:TOK],
                                  start=(kc == 0), stop=(kc == DC - 1))
                if m == 0 and kc == 0:
                    ins.then_inc(sem.panel_used, 1)
            ins.then_inc(sem.act_bank_filled, 1)
            cnt.next("act_bank")


def project_scalar(act, cnt, sem, k, l):
    for c in range(PROJ1 // P):
        t0 = tokens_of(l, c)
        act.wait_ge(sem.act_bank_filled, cnt.next("act_bank"))
        bank = k.bank["act"][(cnt["act_bank"] - 1) % BANKS]
        act.activation(k.p[:, c, t0:TOK], bank[:, t0:TOK], ACT.Copy).then_inc(sem.act_bank_free, 1)
    act.wait_ge(sem.act_bank_free, BANKS + cnt["act_bank"])
    act.nop().then_inc(sem.p_ready, 1)
    cnt.next("p_ready given")


def rope_tensor(pe, cnt, sem, k):
    pe.wait_ge(sem.act_bank_free, BANKS + cnt["act_bank"])
    for j in range(4):
        pe.wait_ge(sem.dve_bank_free, cnt["dve_bank"] + 1)
        bank = k.bank["dve"][cnt["dve_bank"] % BANKS]
        for m in range(2):
            ins = pe.matmul(bank[:, m * 256:m * 256 + 256], k.c1["rot"], k.p[:, 2 * j + m, CTX:TOK],
                              start=True, stop=True)
        ins.then_inc(sem.dve_bank_filled, 1)
        cnt.next("dve_bank")


def rope_vector(dve, cnt, sem, k):
    dve.wait_ge(sem.p_ready, cnt.next("p_ready"))
    bc = lambda n: k.c1[n].unsqueeze(1).to_broadcast([P, 2, SEQ])
    for j in range(4):
        dve.wait_ge(sem.dve_bank_filled, cnt.next("dve_bank"))
        bank = k.bank["dve"][(cnt["dve_bank"] - 1) % BANKS]
        x = k.p[:, 2 * j:2 * j + 2, CTX:TOK]
        tmp = k.tmp[:, 0:512].rearrange("p (c t) -> p c t", c=2)
        dve.tensor_tensor(tmp, bank.rearrange("p (c t) -> p c t", c=2), bc("sin"), ALU.mult).then_inc(sem.dve_bank_free, 1)
        dve.tensor_tensor(x, x, bc("cos"), ALU.mult).then_inc(sem.dve_done, 1)
        dve.wait_ge(sem.dve_done, cnt.next("dve_done"))
        dve.wait_ge(sem.dve_bank_free, BANKS + cnt["dve_bank"])
        dve.tensor_tensor(x, x, tmp, ALU.add).then_inc(sem.dve_done, 1)
        dve.wait_ge(sem.dve_done, cnt.next("dve_done"))
    dve.nop().then_inc(sem.rope_ready, 1)
    cnt.next("rope_ready given")


def lambda_vector(dve, cnt, sem, k, l):
    lam = k.lamrow[0:1, l * 256:l * 256 + 256].rearrange("p (a b d) -> p a b d", a=2, b=2)
    prod = k.tmp[0:1, 0:128].rearrange("p (a d) -> p a d", a=2)
    dve.tensor_tensor(prod, lam[:, :, 0, :], lam[:, :, 1, :], ALU.mult).then_inc(sem.dve_done, 1)
    dve.wait_ge(sem.dve_done, cnt.next("dve_done"))
    dve.tensor_reduce(k.lamsum[0:1, 0:2], prod, AX, ALU.add).then_inc(sem.lam_dots_ready, 1)
    dve.wait_ge(sem.lam_dots_ready, cnt.next("lam_dots_ready given"))
    dve.wait_ge(sem.lam_exp_ready, cnt.next("lam_exp_ready"))
    init = 0.8 - 0.6 * math.exp(-0.3 * l)
    dve.tensor_tensor(k.lamsum[0:1, 2:3], k.lamsum[0:1, 1:2], k.lamsum[0:1, 0:1], ALU.subtract).then_inc(sem.dve_done, 1)
    dve.wait_ge(sem.dve_done, cnt.next("dve_done"))
    dve.tensor_scalar(k.lamsum[0:1, 2:3], k.lamsum[0:1, 2:3], -init, None, ALU.add).then_inc(sem.lam_row_ready, 1)
    dve.wait_ge(sem.lam_row_ready, cnt.next("lam_row_ready given"))
    dve.wait_ge(sem.dve_bank_filled, cnt.next("dve_bank"))
    bank = k.bank["dve"][(cnt["dve_bank"] - 1) % BANKS]
    dve.tensor_copy(k.neglam[:, :], bank[:, 0:1]).then_inc(sem.dve_bank_free, 1)
    dve.wait_ge(sem.dve_bank_free, BANKS + cnt["dve_bank"])


def lambda_scalar(act, cnt, sem, k):
    act.wait_ge(sem.lam_dots_ready, cnt.next("lam_dots_ready"))
    act.activation(k.lamsum[0:1, 0:2], k.lamsum[0:1, 0:2], ACT.Exp).then_inc(sem.lam_exp_ready, 1)
    act.wait_ge(sem.lam_exp_ready, cnt.next("lam_exp_ready given"))


def lambda_tensor(pe, cnt, sem, k):
    pe.wait_ge(sem.lam_row_ready, cnt.next("lam_row_ready"))
    pe.wait_ge(sem.dve_bank_free, cnt["dve_bank"] + 1)
    bank = k.bank["dve"][cnt["dve_bank"] % BANKS]
    pe.matmul(bank[:, 0:1], k.ones[0:1, :], k.lamsum[0:1, 2:3], start=True, stop=True).then_inc(sem.dve_bank_filled, 1)
    cnt.next("dve_bank")


def values_tensor(pe, cnt, sem, k):
    for t in range(4):
        pe.wait_ge(sem.act_bank_free, cnt["act_bank"] + 1)
        bank = k.bank["act"][cnt["act_bank"] % BANKS]
        for h in range(HA):
            ins = pe.transpose(bank[:, h * P:(h + 1) * P], k.p[:, VA + h, t * P:(t + 1) * P], k.ident)
        ins.then_inc(sem.act_bank_filled, 1)
        cnt.next("act_bank")


def values_scalar(act, cnt, sem, k):
    for t in range(4):
        act.wait_ge(sem.act_bank_filled, cnt.next("act_bank"))
        bank = k.bank["act"][(cnt["act_bank"] - 1) % BANKS]
        act.activation(k.vt[:, t, :], bank, ACT.Copy).then_inc(sem.act_bank_free, 1)


ADA_IN_ATTENTION = 9


def attention_items(l):
    return [(h, q) for h in range(HA) for q in range(2 if l == DEPTH - 1 else 0, 4)]


def keys_of(q):
    return 2 if q < 2 else 4


def attention_tensor(pe, cnt, sem, k, l):
    items = attention_items(l)

    def scores(i):
        h, q = items[i]
        n = keys_of(q) * P
        for c in range(2):
            pe.wait_ge(sem.dve_bank_free, cnt["dve_bank"] + 1)
            bank = k.bank["dve"][cnt["dve_bank"] % BANKS]
            rows = slice(c * DHA, (c + 1) * DHA)
            pe.matmul(bank[:, 0:n], k.p[rows, QA + h, q * P:(q + 1) * P],
                                       k.p[rows, KA + h, 0:n], start=True, stop=True).then_inc(sem.dve_bank_filled, 1)
            cnt.next("dve_bank")

    def outputs(i, transposed):
        h, q = items[i]
        nk = keys_of(q)
        pe.wait_ge(sem.act_bank_free, BANKS + transposed)
        pe.wait_ge(sem.act_bank_free, cnt["act_bank"] + 1)
        bank = k.bank["act"][cnt["act_bank"] % BANKS]
        for c in range(nk):
            ins = pe.matmul(bank[:, 0:P], k.vt[:, c, h * P:(h + 1) * P], k.et[:, i % 2, c, :],
                              start=(c == 0), stop=(c == nk - 1))
        ins.then_inc(sem.act_bank_filled, 1)
        cnt.next("act_bank")

    pe.wait_ge(sem.rope_ready, cnt.next("rope_ready"))
    pe.wait_ge(sem.act_bank_free, BANKS + cnt["act_bank"])
    scores(0)
    scores(1)
    transposed = 0
    for i, (h, q) in enumerate(items):
        if i + 2 < len(items):
            scores(i + 2)
        pe.wait_ge(sem.weights_ready, cnt.next("weights_ready"))
        pe.wait_ge(sem.act_bank_free, cnt["act_bank"] + 1)
        bank = k.bank["act"][cnt["act_bank"] % BANKS]
        for c in range(keys_of(q)):
            ins = pe.transpose(bank[:, c * P:(c + 1) * P], k.e[:, i % 2, 0, c * P:(c + 1) * P], k.ident)
        ins.then_inc(sem.act_bank_filled, 1)
        cnt.next("act_bank")
        before, transposed = transposed, cnt["act_bank"]
        if i > 0:
            outputs(i - 1, before)
        if l < DEPTH - 1 and i < ADA_IN_ATTENTION:
            ada_tensor(pe, cnt, sem, k, (i, i + 1))
    outputs(len(items) - 1, transposed)


def attention_scalar(act, cnt, sem, k, l):
    items = attention_items(l)

    def exponentials(i):
        h, q = items[i]
        n = keys_of(q) * P
        act.wait_ge(sem.neg_max_ready, cnt.next("neg_max_ready"))
        s = k.stat[:, i % 2, :]
        for c in range(2):
            src = k.bank["dve"][(k.score_bank[l] + 2 * i + c) % BANKS]
            ins = act.activation(k.e[:, i % 2, c, 0:n], src[:, 0:n], ACT.Exp, bias=s[:, c:c + 1],
                                   scale=DHA ** -0.5, accum_out=s[:, 2 + c:3 + c])
            ins.then_inc(sem.act_done, 1)
            act.wait_ge(sem.act_done, cnt.next("act_done"))
        act.nop().then_inc(sem.exp_ready, 1)
        cnt.next("exp_ready given")

    def outputs(i):
        h, q = items[i]
        act.wait_ge(sem.act_bank_filled, cnt.next("act_bank"))
        bank = k.bank["act"][(cnt["act_bank"] - 1) % BANKS]
        act.activation(k.o[:, h, q * P:(q + 1) * P], bank[:, 0:P], ACT.Copy).then_inc(sem.act_bank_free, 1)

    exponentials(0)
    exponentials(1)
    for i, (h, q) in enumerate(items):
        act.wait_ge(sem.act_bank_filled, cnt.next("act_bank"))
        bank = k.bank["act"][(cnt["act_bank"] - 1) % BANKS]
        act.activation(k.et[:, i % 2, 0:keys_of(q), :],
                                            bank[:, 0:keys_of(q) * P].rearrange("p (c t) -> p c t", t=P), ACT.Copy).then_inc(sem.act_bank_free, 1)
        if i + 2 < len(items):
            exponentials(i + 2)
        if i > 0:
            outputs(i - 1)
        if l < DEPTH - 1 and i < ADA_IN_ATTENTION:
            ada_scalar(act, cnt, sem, k, (i, i + 1))
        hgrn_gates_scalar(act, cnt, sem, k, l, i)
    outputs(len(items) - 1)
    act.wait_ge(sem.act_bank_free, BANKS + cnt["act_bank"])
    act.nop().then_inc(sem.att_ready, 1)
    cnt.next("att_ready given")


def attention_vector(dve, cnt, sem, k, l):
    items = attention_items(l)

    def maxima(i):
        st = k.stat[:, i % 2, :]
        for c in range(2):
            dve.wait_ge(sem.dve_bank_filled, cnt.next("dve_bank"))
            bank = k.bank["dve"][(cnt["dve_bank"] - 1) % BANKS]
            dve.tensor_reduce(st[:, c:c + 1], bank[:, 0:keys_of(items[i][1]) * P], AX, ALU.max).then_inc(sem.dve_done, 1)
            dve.wait_ge(sem.dve_done, cnt.next("dve_done"))
        dve.tensor_scalar(st[:, 0:2], st[:, 0:2], -DHA ** -0.5, None, ALU.mult).then_inc(sem.neg_max_ready, 1)
        dve.wait_ge(sem.neg_max_ready, cnt.next("neg_max_ready given"))

    maxima(0)
    maxima(1)
    for i, (h, q) in enumerate(items):
        n = keys_of(q) * P
        st = k.stat[:, i % 2, :]
        dve.wait_ge(sem.exp_ready, cnt.next("exp_ready"))
        dve.reciprocal(st[:, 4:5], st[:, 2:3]).then_inc(sem.dve_bank_free, 1)
        dve.reciprocal(st[:, 5:6], st[:, 3:4]).then_inc(sem.dve_bank_free, 1)
        dve.wait_ge(sem.dve_bank_free, BANKS + cnt["dve_bank"] - (2 if i + 1 < len(items) else 0))
        dve.tensor_tensor(st[:, 5:6], st[:, 5:6], k.neglam[:, :], ALU.mult).then_inc(sem.dve_done, 1)
        dve.wait_ge(sem.dve_done, cnt.next("dve_done"))
        e0, e1 = k.e[:, i % 2, 0, 0:n], k.e[:, i % 2, 1, 0:n]
        dve.tensor_scalar(e0, e0, st[:, 4:5], None, ALU.mult).then_inc(sem.dve_done, 1)
        dve.wait_ge(sem.dve_done, cnt.next("dve_done"))
        dve.scalar_tensor_tensor(e0, e1, st[:, 5:6], e0, ALU.mult, ALU.add).then_inc(sem.weights_ready, 1)
        dve.wait_ge(sem.weights_ready, cnt.next("weights_ready given"))
        if i + 2 < len(items):
            maxima(i + 2)


def head_norm_vector(dve, cnt, sem, k, l, step):
    t0 = tokens_of(l)
    init = 0.8 - 0.6 * math.exp(-0.3 * l)
    x, sq = k.o[:, :, t0:TOK], k.sq[:, :, t0:TOK]
    if step == 0:
        dve.tensor_tensor(sq, x, x, ALU.mult).then_inc(sem.squares_ready, 1)
        dve.wait_ge(sem.squares_ready, cnt.next("squares_ready given"))
    elif step == 1:
        for c in range(HA):
            dve.wait_ge(sem.dve_bank_filled, cnt.next("dve_bank"))
            bank = k.bank["dve"][(cnt["dve_bank"] - 1) % BANKS]
            dve.tensor_scalar(sq[:, c, :], bank[:, 0:TOK - t0], 1.0 / DVA, EPS, ALU.mult, ALU.add).then_inc(sem.dve_bank_free, 1)
        dve.wait_ge(sem.dve_bank_free, BANKS + cnt["dve_bank"])
        dve.nop().then_inc(sem.mean_square_ready, 1)
        cnt.next("mean_square_ready given")
    elif step == 2:
        dve.wait_ge(sem.root_ready, cnt.next("root_ready"))
        dve.reciprocal(sq, sq).then_inc(sem.dve_done, 1)
        dve.wait_ge(sem.dve_done, cnt.next("dve_done"))
    elif step == 3:
        dve.tensor_tensor(x, x, sq, ALU.mult).then_inc(sem.dve_done, 1)
        dve.wait_ge(sem.dve_done, cnt.next("dve_done"))
    elif step == 4:
        dve.tensor_scalar(k.mix[:, 0:4, t0:TOK], x, k.v1(l, "subln"), 1.0 - init, ALU.mult, ALU.mult).then_inc(sem.dve_done, 1)
        dve.wait_ge(sem.dve_done, cnt.next("dve_done"))


def hgrn_gates_scalar(act, cnt, sem, k, l, step):
    if step < 4:
        act.activation(k.hk[:, step, :], k.p[:, ZF + step, :], ACT.Sigmoid, scale=-1.0)
    elif step == 4:
        act.activation(k.lbd[:, :], k.lbdiff[:, :], ACT.Sigmoid).then_inc(sem.act_done, 1)
        act.wait_ge(sem.act_done, cnt.next("act_done"))
        act.activation(k.p[:, ZF:ZF + 4, :], k.p[:, ZF:ZF + 4, :], ACT.Sigmoid).then_inc(sem.gates_ready, 1)
        act.wait_ge(sem.gates_ready, cnt.next("gates_ready given"))
    elif step == 5:
        hgrn_silu_scalar(act, cnt, sem, k, l)


def lower_bound_vector(dve, cnt, sem, k):
    lb = k.v1(0, "lb")
    dve.tensor_tensor(k.lbdiff[:, :], lb[:, 4:8], lb[:, 0:4], ALU.subtract).then_inc(sem.lbdiff_ready, 1)
    dve.wait_ge(sem.lbdiff_ready, cnt.next("lbdiff_ready given"))


def hgrn_gates_vector(dve, cnt, sem, k, l):
    dve.wait_ge(sem.gates_ready, cnt.next("gates_ready"))
    if l > 0:
        dve.tensor_scalar(k.oml[:, :], k.lbd[:, :], -1.0, 1.0, ALU.mult, ALU.add).then_inc(sem.dve_done, 1)
        dve.wait_ge(sem.dve_done, cnt.next("dve_done"))
        for j in range(4):
            dve.tensor_scalar(k.p[:, ZF + j, :], k.p[:, ZF + j, :], k.oml[:, j:j + 1], k.lbd[:, j:j + 1],
                                ALU.mult, ALU.add)
            ins = dve.tensor_scalar(k.hk[:, j, :], k.hk[:, j, :], k.oml[:, j:j + 1], None, ALU.mult)
        ins.then_inc(sem.dve_done, 1)
        dve.wait_ge(sem.dve_done, cnt.next("dve_done"))


LEVELS = [2, 4, 8, 16, 32, 64, 128]


def pairs_of(l):
    return range(1 if l == DEPTH - 1 else 0, 2)


def halves(ap, size):
    return ap.rearrange("p c (n h b) -> p (c n) h b", h=2, b=size // 2)


def hgrn_tensor(pe, cnt, sem, k, l):
    pe.wait_ge(sem.diagonal_ready, cnt.next("diagonal_ready"))
    k.hgrn_bank[l] = cnt["dve_bank"]
    for tp in pairs_of(l):
        for p in range(2):
            rows = slice(p * 64, p * 64 + 64)
            pe.wait_ge(sem.dve_bank_free, cnt["dve_bank"] + 1)
            bank = k.bank["dve"][cnt["dve_bank"] % BANKS]
            for j in range(4):
                t, g = 2 * tp + j // 2, j % 2
                ts = slice(t * P, (t + 1) * P)
                ins = pe.matmul(bank[:, j * P:(j + 1) * P], k.ksum[rows, g, ts], k.p[rows, QH + g, ts],
                                  start=True, stop=True)
            ins.then_inc(sem.dve_bank_filled, 1)
            cnt.next("dve_bank")
    for i, level in enumerate(LEVELS):
        for direction in range(2):
            if l < DEPTH - 1:
                step = ADA_IN_ATTENTION + 2 * i + direction
                ada_tensor(pe, cnt, sem, k, (step, step + (1 if step < ADA_IN_ATTENTION + 13 else ADA_STEPS - step)))
            if direction == 0:
                pe.wait_ge(sem.forward_factors_ready, cnt.next("forward_factors_ready"))
            else:
                pe.wait_ge(sem.backward_factors_ready, cnt.next("backward_factors_ready"))
            for tp in pairs_of(l):
                for p in range(2):
                    rows = slice(p * 64, p * 64 + 64)
                    pe.wait_ge(sem.dve_bank_free, cnt["dve_bank"] + 1)
                    bank = k.bank["dve"][cnt["dve_bank"] % BANKS]
                    for j in range(4):
                        t, g = 2 * tp + j // 2, j % 2
                        ts = slice(t * P, (t + 1) * P)
                        ins = pe.matmul(bank[:, j * P:(j + 1) * P], k.hk[rows, 2 * direction + g, ts],
                                          k.hq[rows, 2 * direction + g, ts], start=True, stop=True)
                    ins.then_inc(sem.dve_bank_filled, 1)
                    cnt.next("dve_bank")
        if i == 0:
            t0 = tokens_of(l)
            group_norm_tensor(pe, cnt, sem, k, k.sq[:, :, t0:TOK], HA, TOK - t0, k.ones)
    for t2 in range(2):
        pe.wait_ge(sem.act_bank_free, cnt["act_bank"] + 1)
        bank = k.bank["act"][cnt["act_bank"] % BANKS]
        for j in range(4):
            t, g = 2 * t2 + j // 2, j % 2
            ins = pe.transpose(bank[:, j * P:(j + 1) * P], k.p[:, IH + g, t * P:(t + 1) * P], k.ident)
        ins.then_inc(sem.act_bank_filled, 1)
        cnt.next("act_bank")
    pe.wait_ge(sem.forward_factors_ready, cnt.next("forward_factors_ready"))
    pe.wait_ge(sem.backward_factors_ready, cnt.next("backward_factors_ready"))
    for direction in range(2):
        for t2 in range(2):
            pe.wait_ge(sem.act_bank_free, cnt["act_bank"] + 1)
            bank = k.bank["act"][cnt["act_bank"] % BANKS]
            for j in range(4):
                t, g = 2 * t2 + j // 2, j % 2
                ins = pe.transpose(bank[:, j * P:(j + 1) * P], k.hk[:, 2 * direction + g, t * P:(t + 1) * P], k.ident)
            ins.then_inc(sem.act_bank_filled, 1)
            cnt.next("act_bank")
    pe.wait_ge(sem.act_bank_free, BANKS + cnt["act_bank"])
    for direction in range(2):
        for t2 in range(2):
            pe.wait_ge(sem.dve_bank_free, cnt["dve_bank"] + 1)
            bank = k.bank["dve"][cnt["dve_bank"] % BANKS]
            for j in range(4):
                t, g = 2 * t2 + j // 2, j % 2
                ins = pe.matmul(bank[:, j * P:(j + 1) * P], k.hkt[:, direction, t, g * P:(g + 1) * P],
                                  k.hvt[:, t, g * P:(g + 1) * P], start=True, stop=True)
            ins.then_inc(sem.dve_bank_filled, 1)
            cnt.next("dve_bank")
    pe.wait_ge(sem.tile_states_ready, cnt.next("tile_states_ready"))
    for g in range(2):
        pe.wait_ge(sem.act_bank_free, cnt["act_bank"] + 1)
        bank = k.bank["act"][cnt["act_bank"] % BANKS]
        for t in range(2 * pairs_of(l)[0], 4):
            ts = slice(t * P, (t + 1) * P)
            for direction in range(2):
                pe.matmul(bank[:, ts], k.hsin[:, direction, t, g, :], k.hq[:, 2 * direction + g, ts],
                            start=(direction == 0), stop=False, skip_group_check=True)
            for p in range(2):
                rows = slice(p * 64, p * 64 + 64)
                ins = pe.matmul(bank[rows, ts], k.hvt[:, t, g * P + p * 64:g * P + p * 64 + 64],
                                  k.ha[:, t // 2, p, (t % 2) * 2 + g, :], start=False, stop=True,
                                  skip_group_check=True)
        ins.then_inc(sem.act_bank_filled, 1)
        cnt.next("act_bank")


def hgrn_scalar(act, cnt, sem, k, l):
    if l < DEPTH - 1:
        ada_scalar(act, cnt, sem, k, (ADA_IN_ATTENTION, ADA_IN_ATTENTION + 2))
    root_scalar(act, cnt, sem, k, k.sq[:, :, tokens_of(l):TOK])
    if l < DEPTH - 1:
        ada_scalar(act, cnt, sem, k, (ADA_IN_ATTENTION + 2, ADA_STEPS))
    for t2 in range(2):
        act.wait_ge(sem.act_bank_filled, cnt.next("act_bank"))
        bank = k.bank["act"][(cnt["act_bank"] - 1) % BANKS]
        act.activation(k.hvt[:, 2 * t2:2 * t2 + 2, :],
                                            bank.rearrange("p (t n) -> p t n", t=2), ACT.Copy).then_inc(sem.act_bank_free, 1)
    for direction in range(2):
        for t2 in range(2):
            act.wait_ge(sem.act_bank_filled, cnt.next("act_bank"))
            bank = k.bank["act"][(cnt["act_bank"] - 1) % BANKS]
            act.activation(k.hkt[:, direction, 2 * t2:2 * t2 + 2, :],
                                                bank.rearrange("p (t n) -> p t n", t=2), ACT.Copy).then_inc(sem.act_bank_free, 1)


def hgrn_vector(dve, cnt, sem, k, l):
    q, f = k.p[:, QH:QH + 2, :], k.p[:, ZB:ZB + 2, :]
    qb, kb = k.hq[:, 2:4, :], k.hk[:, 2:4, :]
    dve.wait_ge(sem.att_ready, cnt.next("att_ready"))
    dve.nop().then_inc(sem.attention_over, 1)
    dve.tensor_tensor(k.ksum, k.hk[:, 0:2, :], kb, ALU.add).then_inc(sem.diagonal_ready, 1)
    dve.wait_ge(sem.diagonal_ready, cnt.next("diagonal_ready given"))
    t0 = tokens_of(l)
    dve.tensor_tensor(qb[:, :, t0:], q[:, :, t0:], f[:, :, t0:], ALU.mult).then_inc(sem.backward_factors_ready, 1)
    dve.wait_ge(sem.backward_factors_ready, cnt.next("backward_factors_ready given"))
    head_norm_vector(dve, cnt, sem, k, l, 0)
    for tp in pairs_of(l):
        for p in range(2):
            dve.wait_ge(sem.dve_bank_filled, cnt.next("dve_bank"))
            bank = k.bank["dve"][(cnt["dve_bank"] - 1) % BANKS]
            dve.tensor_copy(k.ha[:, tp, p], bank.rearrange("p (j n) -> p j n", j=4)).then_inc(sem.dve_bank_free, 1)
    dve.wait_ge(sem.masks_loaded, 16 * (l + 1))
    for i, level in enumerate(LEVELS):
        for direction in range(2):
            dve.wait_ge(sem.dve_bank_free, BANKS + cnt["dve_bank"])
            mask = k.hmask[:, direction, i, :].bitcast(U32).unsqueeze(1).to_broadcast([P, 4, P])
            for tp in pairs_of(l):
                for p in range(2):
                    dve.wait_ge(sem.dve_bank_filled, cnt.next("dve_bank"))
                    bank = k.bank["dve"][(cnt["dve_bank"] - 1) % BANKS]
                    if direction == 1 and tp == 1 and p == 1:
                        qh, kh, fh = halves(qb, level), halves(kb, level), halves(f, level)
                        if l < DEPTH - 1:
                            n = slice(0, 2 * TOK // level)
                            dve.tensor_tensor(qh[:, n, 0, :], qh[:, n, 0, :],
                                                       fh[:, n, 1, 0:1].to_broadcast([P, 2 * TOK // level, level // 2]),
                                                       ALU.mult).then_inc(sem.dve_done, 1)
                            dve.wait_ge(sem.dve_done, cnt.next("dve_done"))
                        else:
                            for g in range(2):
                                n = slice(g * TOK // level + CTX // level, (g + 1) * TOK // level)
                                ins = dve.tensor_tensor(qh[:, n, 0, :], qh[:, n, 0, :],
                                                          fh[:, n, 1, 0:1].to_broadcast([P, SEQ // level, level // 2]),
                                                          ALU.mult)
                            ins.then_inc(sem.dve_done, 1)
                            dve.wait_ge(sem.dve_done, cnt.next("dve_done"))
                        dve.tensor_tensor(kh[:, :, 1, :], kh[:, :, 1, :],
                                                   fh[:, :, 0, 0:1].to_broadcast([P, 2 * TOK // level, level // 2]),
                                                   ALU.mult).then_inc(sem.dve_done, 1)
                        dve.wait_ge(sem.dve_done, cnt.next("dve_done"))
                        dve.tensor_tensor(fh[:, :, 0, 0], fh[:, :, 0, 0], fh[:, :, 1, 0], ALU.mult).then_inc(sem.backward_factors_ready, 1)
                        dve.wait_ge(sem.backward_factors_ready, cnt.next("backward_factors_ready given"))
                    dve.copy_predicated(k.ha[:, tp, p], mask,
                                                             bank.rearrange("p (j n) -> p j n", j=4)).then_inc(sem.dve_bank_free, 1)
        head_norm_vector(dve, cnt, sem, k, l, i + 1)
    block = k.c1["block"].unsqueeze(1).to_broadcast([P, 4, P])
    dve.memset(k.hsin, 0.0).then_inc(sem.dve_done, 1)
    dve.wait_ge(sem.dve_done, cnt.next("dve_done"))
    for direction in range(2):
        for t2 in range(2):
            dve.wait_ge(sem.dve_bank_filled, cnt.next("dve_bank"))
            bank = k.bank["dve"][(cnt["dve_bank"] - 1) % BANKS]
            dve.tensor_tensor(k.hdel[:, direction, t2], bank.rearrange("p (j n) -> p j n", j=4),
                                                   block, ALU.mult).then_inc(sem.dve_bank_free, 1)
    dve.wait_ge(sem.dve_bank_free, BANKS + cnt["dve_bank"])
    dve.wait_ge(sem.forward_total_ready, cnt.next("forward_total_ready"))
    for step in range(3):
        for direction, order in enumerate(((0, 1, 2, 3), (1, 0, 3, 2))):
            t, nxt = order[step], order[step + 1]
            for g in range(2):
                decay = k.p[:, ZF + 2 * direction + g, t * P:t * P + 1]
                ins = dve.scalar_tensor_tensor(k.hsin[:, direction, nxt, g, :], k.hsin[:, direction, t, g, :], decay,
                                                 k.hdel[:, direction, t // 2, (t % 2) * 2 + g, :], ALU.mult, ALU.add)
        ins.then_inc(sem.dve_done, 1)
        dve.wait_ge(sem.dve_done, cnt.next("dve_done"))
    dve.nop().then_inc(sem.tile_states_ready, 1)
    cnt.next("tile_states_ready given")


def hgrn_pool(pool, cnt, sem, k, l):
    pool.wait_ge(sem.attention_over, cnt.next("attention_over"))
    t0 = tokens_of(l)
    q, f = k.p[:, QH:QH + 2, :], k.p[:, ZF:ZF + 2, :]
    qf, kf = k.hq[:, 0:2, :], k.hk[:, 0:2, :]
    pool.dma_start(k.hmask, k.a["masks"].rearrange("p (d i n) -> p d i n", d=2, i=7)).then_inc(sem.masks_loaded, 16)
    pool.tensor_tensor(qf[:, :, t0:], q[:, :, t0:], f[:, :, t0:], ALU.mult).then_inc(sem.forward_factors_ready, 1)
    pool.wait_ge(sem.forward_factors_ready, cnt.next("forward_factors_ready given"))
    per = 2 * len(pairs_of(l))
    for i, level in enumerate(LEVELS):
        pool.wait_ge(sem.dve_bank_filled, k.hgrn_bank[l] + per * (2 + 2 * i) + (HA if i > 0 else 0))
        qh, kh, fh = halves(qf, level), halves(kf, level), halves(f, level)
        if l < DEPTH - 1:
            pool.tensor_tensor(qh[:, :, 1, :], qh[:, :, 1, :],
                                         fh[:, :, 0, 0:1].to_broadcast([P, 2 * TOK // level, level // 2]), ALU.mult).then_inc(sem.pool_done, 1)
            pool.wait_ge(sem.pool_done, cnt.next("pool_done"))
        else:
            for g in range(2):
                n = slice(g * TOK // level + CTX // level, (g + 1) * TOK // level)
                pool.tensor_tensor(qh[:, n, 1, :], qh[:, n, 1, :],
                                             fh[:, n, 0, 0:1].to_broadcast([P, SEQ // level, level // 2]), ALU.mult).then_inc(sem.pool_done, 1)
                pool.wait_ge(sem.pool_done, cnt.next("pool_done"))
        pool.tensor_tensor(kh[:, :, 0, :], kh[:, :, 0, :],
                                     fh[:, :, 1, 0:1].to_broadcast([P, 2 * TOK // level, level // 2]), ALU.mult).then_inc(sem.pool_done, 1)
        pool.wait_ge(sem.pool_done, cnt.next("pool_done"))
        pool.tensor_tensor(fh[:, :, 0, 0], fh[:, :, 0, 0], fh[:, :, 1, 0], ALU.mult).then_inc(sem.forward_factors_ready, 1)
        pool.wait_ge(sem.forward_factors_ready, cnt.next("forward_factors_ready given"))
    pool.nop().then_inc(sem.forward_total_ready, 1)


def hgrn_out_scalar(act, cnt, sem, k, l):
    t0 = tokens_of(l)
    for g in range(2):
        act.wait_ge(sem.act_bank_filled, cnt.next("act_bank"))
        bank = k.bank["act"][(cnt["act_bank"] - 1) % BANKS]
        act.activation(k.o[:, g, t0:TOK], bank[:, t0:TOK], ACT.Copy).then_inc(sem.act_bank_free, 1)
    act.wait_ge(sem.act_bank_free, BANKS + cnt["act_bank"])
    act.nop().then_inc(sem.rec_ready, 1)
    cnt.next("rec_ready given")


def hgrn_out_vector(dve, cnt, sem, k, l):
    t0 = tokens_of(l)
    dve.wait_ge(sem.rec_ready, cnt.next("rec_ready"))
    x, sq = k.o[:, 0:2, t0:TOK], k.sq[:, 0:2, t0:TOK]
    group_norm_vector(dve, cnt, sem, k, x, sq, 2, TOK - t0, 64, EPS)
    dve.wait_ge(sem.silu_ready, cnt.next("silu_ready"))
    dve.scalar_tensor_tensor(k.mix[:, 4:6, t0:TOK], x, k.v1(l, "hnorm"), k.p[:, GH:GH + 2, t0:TOK],
                                      ALU.mult, ALU.mult).then_inc(sem.dve_done, 1)
    dve.wait_ge(sem.dve_done, cnt.next("dve_done"))


def hgrn_silu_scalar(act, cnt, sem, k, l):
    t0 = tokens_of(l)
    act.activation(k.p[:, GH:GH + 2, t0:TOK], k.p[:, GH:GH + 2, t0:TOK], ACT.Silu).then_inc(sem.silu_ready, 1)
    act.wait_ge(sem.silu_ready, cnt.next("silu_ready given"))


def fourier_tensor(pe, cnt, sem, k, l):
    s0 = 1 if l == DEPTH - 1 else 0
    for t in range(2 * s0, 4):
        pe.wait_ge(sem.act_bank_free, cnt["act_bank"] + 1)
        bank = k.bank["act"][cnt["act_bank"] % BANKS]
        for c in range(2):
            ins = pe.matmul(bank[:, c * 256:c * 256 + 256], k.p[:, UF + c, t * P:(t + 1) * P], k.c1["dftd"],
                              start=True, stop=True)
        ins.then_inc(sem.act_bank_filled, 1)
        cnt.next("act_bank")
    pe.wait_ge(sem.act_bank_free, BANKS + cnt["act_bank"])
    dt = k.c1["dftt"].rearrange("p (t s n) -> p t s n", t=2, s=2)
    for c in range(2):
        for s in range(s0, 2):
            pe.wait_ge(sem.act_bank_free, cnt["act_bank"] + 1)
            bank = k.bank["act"][cnt["act_bank"] % BANKS]
            n = 0
            for t in range(2):
                for cs in range(2):
                    ins = pe.matmul(bank[:, 0:SEQ], k.fa[:, 2 * s + t, c, cs * P:(cs + 1) * P], dt[:, t, cs, :],
                                      start=(n == 0), stop=(n == 3))
                    n += 1
            ins.then_inc(sem.act_bank_filled, 1)
            cnt.next("act_bank")
    pe.wait_ge(sem.act_bank_free, BANKS + cnt["act_bank"])
    pe.wait_ge(sem.panel_loaded[cnt["panel"] % RING], k.panel_value[cnt["panel"]])
    panel = k.panel(cnt.next("panel") - 1)
    t0 = tokens_of(l)
    for m in range(2):
        pe.wait_ge(sem.act_bank_free, cnt["act_bank"] + 1)
        bank = k.bank["act"][cnt["act_bank"] % BANKS]
        for kc in range(2):
            ins = pe.matmul(bank[:, t0:TOK], panel[:, kc, m * P:(m + 1) * P], k.fy[:, kc, t0:TOK],
                              start=(kc == 0), stop=(kc == 1))
            if m == 0 and kc == 0:
                ins.then_inc(sem.panel_used, 1)
        ins.then_inc(sem.act_bank_filled, 1)
        cnt.next("act_bank")


def fourier_scalar(act, cnt, sem, k, l):
    s0 = 1 if l == DEPTH - 1 else 0
    for t in range(2 * s0, 4):
        act.wait_ge(sem.act_bank_filled, cnt.next("act_bank"))
        bank = k.bank["act"][(cnt["act_bank"] - 1) % BANKS]
        act.activation(k.fa[:, t, :, :], bank.rearrange("p (c n) -> p c n", c=2), ACT.Copy).then_inc(sem.act_bank_free, 1)
    for c in range(2):
        for s in range(s0, 2):
            act.wait_ge(sem.act_bank_filled, cnt.next("act_bank"))
            bank = k.bank["act"][(cnt["act_bank"] - 1) % BANKS]
            act.activation(k.fy[:, c, s * SEQ:(s + 1) * SEQ], bank[:, 0:SEQ], ACT.Copy).then_inc(sem.act_bank_free, 1)
    t0 = tokens_of(l)
    for m in range(2):
        act.wait_ge(sem.act_bank_filled, cnt.next("act_bank"))
        bank = k.bank["act"][(cnt["act_bank"] - 1) % BANKS]
        act.activation(k.mix[:, 6 + m, t0:TOK], bank[:, t0:TOK], ACT.Copy).then_inc(sem.act_bank_free, 1)
    act.wait_ge(sem.act_bank_free, BANKS + cnt["act_bank"])


def merge_tensor(pe, cnt, sem, k, l):
    pe.wait_ge(sem.mix_ready, cnt.next("mix_ready"))
    pe.wait_ge(sem.act_bank_free, BANKS + cnt["act_bank"])
    t0 = tokens_of(l)
    for j in range(4):
        pe.wait_ge(sem.panel_loaded[cnt["panel"] % RING], k.panel_value[cnt["panel"]])
        panel = k.panel(cnt.next("panel") - 1)
        for m in range(2):
            pe.wait_ge(sem.dve_bank_free, cnt["dve_bank"] + 1)
            bank = k.bank["dve"][cnt["dve_bank"] % BANKS]
            for kc in range(DC):
                ins = pe.matmul(bank[:, t0:TOK], panel[:, kc, m * P:(m + 1) * P], k.mix[:, kc, t0:TOK],
                                  start=(kc == 0), stop=(kc == DC - 1))
                if m == 0 and kc == 0:
                    ins.then_inc(sem.panel_used, 1)
            ins.then_inc(sem.dve_bank_filled, 1)
            cnt.next("dve_bank")


def residual_vector(dve, cnt, sem, k, l, gate):
    for c in range(DC):
        dve.wait_ge(sem.dve_bank_filled, cnt.next("dve_bank"))
        bank = k.bank["dve"][(cnt["dve_bank"] - 1) % BANKS]
        for s in range(2 if tokens_of(l) == 0 else 1):
            s = 1 - s
            x = k.x[:, c, s * SEQ:(s + 1) * SEQ]
            ins = dve.scalar_tensor_tensor(x, bank[:, s * SEQ:(s + 1) * SEQ], k.mod[:, gate + c, s:s + 1], x,
                                             ALU.mult, ALU.add)
        ins.then_inc(sem.dve_bank_free, 1)
    dve.wait_ge(sem.dve_bank_free, BANKS + cnt["dve_bank"])


def ffn_up_tensor(pe, cnt, sem, k, l):
    t0 = tokens_of(l)
    for j in range(FC // 2):
        for part in range(2):
            pe.wait_ge(sem.panel_loaded[cnt["panel"] % RING], k.panel_value[cnt["panel"]])
            panel = k.panel(cnt.next("panel") - 1)
            for m in range(2):
                pe.wait_ge(sem.act_bank_free, cnt["act_bank"] + 1)
                bank = k.bank["act"][cnt["act_bank"] % BANKS]
                for kc in range(DC):
                    if j == 0 and part == 0 and m == 0:
                        pe.wait_ge(sem.xn_ready, cnt.next("xn_ready"))
                    ins = pe.matmul(bank[:, t0:TOK], panel[:, kc, m * P:(m + 1) * P], k.xn[:, kc, t0:TOK],
                                      start=(kc == 0), stop=(kc == DC - 1))
                    if m == 0 and kc == 0:
                        ins.then_inc(sem.panel_used, 1)
                ins.then_inc(sem.act_bank_filled, 1)
                cnt.next("act_bank")


def ffn_up_scalar(act, cnt, sem, k, l):
    t0 = tokens_of(l)
    for j in range(FC // 2):
        if j >= 2:
            act.wait_ge(sem.up_used, cnt.next("up_used"))
        for m in range(4):
            act.wait_ge(sem.act_bank_filled, cnt.next("act_bank"))
            bank = k.bank["act"][(cnt["act_bank"] - 1) % BANKS]
            act.activation(k.u[:, j % 2, m, t0:TOK], bank[:, t0:TOK], ACT.Copy).then_inc(sem.act_bank_free, 1)
        act.wait_ge(sem.act_bank_free, BANKS + cnt["act_bank"])
        act.nop().then_inc(sem.up_ready, 1)
        cnt.next("up_ready given")
        act.wait_ge(sem.conv_ready, cnt.next("conv_ready"))
        g = k.cv[:, j % 2, 0:2, t0:TOK]
        act.activation(g, g, ACT.Silu).then_inc(sem.gate_ready, 1)
        act.wait_ge(sem.gate_ready, cnt.next("gate_ready given"))
    act.wait_ge(sem.up_used, cnt.next("up_used", 2))


def ffn_up_vector(dve, cnt, sem, k, l):
    t0 = tokens_of(l)
    n = (TOK - t0) // SEQ
    seg = lambda ap: ap.rearrange("p (s t) -> p s t", s=n)

    def finish(j):
        dve.wait_ge(sem.gate_ready, cnt.next("gate_ready"))
        dve.tensor_tensor(k.h[:, 2 * j:2 * j + 2, t0:TOK], k.cv[:, j % 2, 0:2, t0:TOK],
                                   k.cv[:, j % 2, 2:4, t0:TOK], ALU.mult).then_inc(sem.dve_done, 1)
        dve.wait_ge(sem.dve_done, cnt.next("dve_done"))

    for j in range(FC // 2):
        dve.wait_ge(sem.up_ready, cnt.next("up_ready"))
        for step in range(3):
            for m in range(4):
                c = (2 * j + m) if m < 2 else (FC + 2 * j + m - 2)
                u, o = seg(k.u[:, j % 2, m, t0:TOK]), seg(k.cv[:, j % 2, m, t0:TOK])
                w = lambda tap: k.conv(l, tap, c)
                if step == 0:
                    ins = dve.tensor_scalar(o, u, w(1), w(3), ALU.mult, ALU.add)
                elif step == 1:
                    ins = dve.scalar_tensor_tensor(o[:, :, 1:], u[:, :, :-1], w(0), o[:, :, 1:], ALU.mult, ALU.add)
                else:
                    ins = dve.scalar_tensor_tensor(o[:, :, :-1], u[:, :, 1:], w(2), o[:, :, :-1], ALU.mult, ALU.add)
            ins.then_inc(sem.dve_done, 1)
            dve.wait_ge(sem.dve_done, cnt.next("dve_done"))
        dve.nop().then_inc(sem.up_used, 1)
        cnt.next("up_used given")
        dve.nop().then_inc(sem.conv_ready, 1)
        cnt.next("conv_ready given")
        if j:
            finish(j - 1)
    finish(FC // 2 - 1)
    dve.nop().then_inc(sem.hidden_ready, 1)
    cnt.next("hidden_ready given")


def ffn_down_tensor(pe, cnt, sem, k, l):
    pe.wait_ge(sem.hidden_ready, cnt.next("hidden_ready"))
    t0 = tokens_of(l)
    for j in range(4):
        banks = []
        for part, rows in enumerate((8, 8, 6)):
            pe.wait_ge(sem.panel_loaded[cnt["panel"] % RING], k.panel_value[cnt["panel"]])
            panel = k.panel(cnt.next("panel") - 1)
            for m in range(2):
                if part == 0:
                    pe.wait_ge(sem.dve_bank_free, cnt["dve_bank"] + m + 1)
                    banks.append(k.bank["dve"][(cnt["dve_bank"] + m) % BANKS])
                for kc in range(rows):
                    kk = part * 8 + kc
                    ins = pe.matmul(banks[m][:, t0:TOK], panel[:, kc, m * P:(m + 1) * P], k.h[:, kk, t0:TOK],
                                      start=(kk == 0), stop=(kk == FC - 1))
                    if m == 0 and kc == 0:
                        ins.then_inc(sem.panel_used, 1)
                if part == 2:
                    ins.then_inc(sem.dve_bank_filled, 1)
                    cnt.next("dve_bank")


def store_features_tensor(pe, cnt, sem, k, src):
    for t in range(2):
        for c0 in range(0, DC, 4):
            pe.wait_ge(sem.act_bank_free, cnt["act_bank"] + 1)
            bank = k.bank["act"][cnt["act_bank"] % BANKS]
            for c in range(4):
                ins = pe.transpose(bank[:, c * P:(c + 1) * P], src[:, c0 + c, t * P:(t + 1) * P], k.ident)
            ins.then_inc(sem.act_bank_filled, 1)
            cnt.next("act_bank")


def store_features_scalar(act, cnt, sem, k, dst):
    for t in range(2):
        for c0 in range(0, 2):
            act.wait_ge(sem.act_bank_filled, cnt.next("act_bank"))
            bank = k.bank["act"][(cnt["act_bank"] - 1) % BANKS]
            act.activation(dst[:, t, c0 * 512:c0 * 512 + 512], bank, ACT.Copy).then_inc(sem.act_bank_free, 1)
    act.wait_ge(sem.act_bank_free, BANKS + cnt["act_bank"])


def wide(ap, c, n):
    return ap.unsqueeze(2).to_broadcast([P, c, n])


def norm2_vector(dve, cnt, sem, k, l, which):
    norm_vector(dve, cnt, sem, k, k.x2, (0, SEQ), k.xn2)
    w = k.v2(l, which)
    for c in range(DC):
        dve.scalar_tensor_tensor(k.xn2[:, c, :], k.x2[:, c, :], w[:, c:c + 1], k.rms[:, 0:SEQ], ALU.mult, ALU.mult
                                   ).then_inc(sem.xn_ready, 1)


PROJECT_STEPS = [(c, ACT.Copy) for c in range(24)] + [(NG, ACT.Sigmoid)] + \
    [(c, ACT.Copy) for c in range(24, 30)] + [(c, ACT.Sigmoid) for c in range(30, 54)]
RWKV_STEPS = (0, 14)
LORA_STEPS = (14, 17)
DECAY_STEPS = (17, 22)
SOLVE_STEPS = (22, 47)
ATTENTION_STEPS = (47, 55)


def project2_tensor(pe, cnt, sem, k, steps):
    for step in range(steps[0], steps[1]):
        chunk = PROJECT_STEPS[step][0]
        cols = IN_G if chunk == NG else PANEL
        rows = min(cols, P)
        m = 0 if chunk == NG else chunk % 2
        if m == 0:
            pe.wait_ge(sem.panel_loaded[cnt["panel"] % RING], k.panel_value[cnt["panel"]])
            cnt.next("panel")
        panel = k.panel(cnt["panel"] - 1, cols)
        pe.wait_ge(sem.act_bank_free, cnt["act_bank"] + 1)
        bank = k.bank["act"][cnt["act_bank"] % BANKS]
        for kc in range(DC):
            if step == 0:
                pe.wait_ge(sem.xn_ready, cnt.next("xn_ready"))
            ins = pe.matmul(bank[0:rows, 0:SEQ], panel[:, kc, m * P:m * P + rows], k.xn2[:, kc, :],
                              start=(kc == 0), stop=(kc == DC - 1))
            if m == 0 and kc == 0:
                ins.then_inc(sem.panel_used, 1)
        ins.then_inc(sem.act_bank_filled, 1)
        cnt.next("act_bank")


def project2_scalar(act, cnt, sem, k, steps):
    for step in range(steps[0], steps[1]):
        c, func = PROJECT_STEPS[step]
        rows = IN_G if c == NG else P
        act.wait_ge(sem.act_bank_filled, cnt.next("act_bank"))
        bank = k.bank["act"][(cnt["act_bank"] - 1) % BANKS]
        act.activation(k.p2[0:rows, c, :], bank[0:rows, 0:SEQ], func).then_inc(sem.act_bank_free, 1)


def rwkv_inputs_vector(dve, cnt, sem, k, l):
    dve.wait_ge(sem.p_ready, cnt.next("p_ready"))
    for c0, c1 in ((ZWA, ZG + 1), (ZR, ZWA)):
        z, t = k.p2[:, c0:c1, :], k.shift[:, c0:c1, :]
        dve.tensor_tensor(t, z, wide(k.v2(l, "mu")[:, c0:c1], c1 - c0, SEQ), ALU.mult).then_inc(sem.dve_done, 1)
        dve.wait_ge(sem.dve_done, cnt.next("dve_done"))
        dve.tensor_tensor(z, z, t, ALU.subtract).then_inc(sem.dve_done, 1)
        dve.wait_ge(sem.dve_done, cnt.next("dve_done"))
        dve.tensor_tensor(z[:, :, 1:], z[:, :, 1:], t[:, :, :-1], ALU.add).then_inc(sem.dve_done, 1)
        dve.wait_ge(sem.dve_done, cnt.next("dve_done"))
        if c0 == ZWA:
            dve.nop().then_inc(sem.shifted_ready, 1)
            cnt.next("shifted_ready given")
    r, zk, v = k.p2[:, ZR:ZR + 4, :], k.p2[:, ZK:ZK + 4, :], k.p2[:, ZV:ZV + 4, :]
    dve.tensor_tensor(k.ap, zk, wide(k.v2(l, "kk"), 4, SEQ), ALU.mult).then_inc(sem.dve_done, 1)
    dve.wait_ge(sem.dve_done, cnt.next("dve_done"))
    group_norm_vector(dve, cnt, sem, k, k.ap, k.ra, 4, SEQ, 1, 0.0, clamp=1e-12)
    dve.wait_ge(sem.lora_ready, cnt.next("lora_ready"))
    dve.tensor_scalar(k.ra, k.bi, -1.0, None, ALU.add).then_inc(sem.dve_done, 1)
    dve.wait_ge(sem.dve_done, cnt.next("dve_done"))
    dve.tensor_tensor(k.ra, k.ra, wide(k.v2(l, "ka"), 4, SEQ), ALU.mult).then_inc(sem.dve_done, 1)
    dve.wait_ge(sem.dve_done, cnt.next("dve_done"))
    dve.scalar_tensor_tensor(zk, k.ra, 1.0, zk, ALU.add, ALU.mult).then_inc(sem.dve_done, 1)
    dve.wait_ge(sem.dve_done, cnt.next("dve_done"))
    dve.tensor_tensor(k.bi, k.bi, k.ap, ALU.mult).then_inc(sem.dve_done, 1)
    dve.wait_ge(sem.dve_done, cnt.next("dve_done"))
    dve.tensor_tensor(k.ra, r, zk, ALU.mult).then_inc(sem.dve_done, 1)
    dve.wait_ge(sem.dve_done, cnt.next("dve_done"))
    dve.tensor_tensor(k.ra, k.ra, wide(k.v2(l, "rk"), 4, SEQ), ALU.mult).then_inc(sem.bonus_ready, 1)
    dve.wait_ge(sem.bonus_ready, cnt.next("bonus_ready given"))
    for c in range(4):
        dve.wait_ge(sem.dve_bank_filled, cnt.next("dve_bank"))
        bank = k.bank["dve"][(cnt["dve_bank"] - 1) % BANKS]
        dve.tensor_tensor(k.bonus[:, c, :], bank[:, 0:SEQ], v[:, c, :], ALU.mult).then_inc(sem.dve_bank_free, 1)
    dve.wait_ge(sem.dve_bank_free, BANKS + cnt["dve_bank"])
    dve.tensor_scalar(k.lw, k.lw, -math.exp(-0.5), None, ALU.mult).then_inc(sem.dve_done, 1)
    dve.wait_ge(sem.dve_done, cnt.next("dve_done"))
    for c in range(4):
        for t in range(2):
            ins = dve.tensor_tensor_scan(k.ra[:, c, t * P:(t + 1) * P], k.ones, k.lw[:, c, t * P:(t + 1) * P], 0.0,
                                           ALU.mult, ALU.add)
    ins.then_inc(sem.dve_done, 1)
    dve.wait_ge(sem.dve_done, cnt.next("dve_done"))
    mid = k.small[:, 0:8].rearrange("p (c t) -> p c t", c=4)
    cum = k.ra.rearrange("p c (t n) -> p c t n", t=2)
    dve.tensor_copy(mid, cum[:, :, :, 63]).then_inc(sem.dve_done, 1)
    dve.wait_ge(sem.dve_done, cnt.next("dve_done"))
    for t in range(2):
        ins = dve.tensor_tensor(cum[:, :, t, :], cum[:, :, t, :], wide(mid[:, :, t], 4, P), ALU.subtract)
    ins.then_inc(sem.dve_done, 1)
    dve.wait_ge(sem.dve_done, cnt.next("dve_done"))
    dve.tensor_tensor(k.lw, k.ra, k.lw, ALU.subtract).then_inc(sem.cum_ready, 1)
    dve.wait_ge(sem.cum_ready, cnt.next("cum_ready given"))
    dve.wait_ge(sem.decays_ready, cnt.next("decays_ready"))
    dve.scalar_tensor_tensor(k.ap, k.ap, -1.0, k.lw, ALU.mult, ALU.mult)
    dve.tensor_tensor(k.bi, k.bi, k.e2, ALU.mult)
    dve.tensor_tensor(zk, zk, k.e2, ALU.mult)
    dve.tensor_tensor(r, r, k.e1, ALU.mult)
    last = k.e1.rearrange("p c (t n) -> p c t n", t=2)[:, :, :, P - 1]
    dve.tensor_copy(k.small[:, 16:24].rearrange("p (c t) -> p c t", c=4), last).then_inc(sem.factors_ready, 1)
    dve.wait_ge(sem.factors_ready, cnt.next("factors_ready given"))


def rwkv_inputs_scalar(act, cnt, sem, k, l):
    act.wait_ge(sem.shifted_ready, cnt.next("shifted_ready"))
    act.activation(k.p2[0:64, ZWA, :], k.p2[0:64, ZWA, :], ACT.Tanh)
    act.activation(k.p2[:, ZG, :], k.p2[:, ZG, :], ACT.Sigmoid).then_inc(sem.lora_in_ready, 1)
    act.wait_ge(sem.lora_in_ready, cnt.next("lora_in_ready given"))
    for dst, bias in ((k.lw, "w0"), (k.bi, "a0"), (k.g, None)):
        for c in range(4):
            act.wait_ge(sem.act_bank_filled, cnt.next("act_bank"))
            bank = k.bank["act"][(cnt["act_bank"] - 1) % BANKS]
            if bias:
                ins = act.activation(dst[:, c, :], bank[:, 0:SEQ], ACT.Sigmoid, bias=k.v2(l, bias)[:, c:c + 1])
            else:
                ins = act.activation(dst[:, c, :], bank[:, 0:SEQ], ACT.Copy)
            ins.then_inc(sem.act_bank_free, 1)
    act.wait_ge(sem.act_bank_free, BANKS + cnt["act_bank"])
    act.nop().then_inc(sem.lora_ready, 1)
    cnt.next("lora_ready given")
    root_scalar(act, cnt, sem, k, k.ra)
    project2_scalar(act, cnt, sem, k, DECAY_STEPS)
    act.wait_ge(sem.cum_ready, cnt.next("cum_ready"))
    act.activation(k.e1, k.ra, ACT.Exp)
    act.activation(k.e2, k.ra, ACT.Exp, scale=-1.0)
    act.activation(k.small[:, 8:16], k.small[:, 0:8], ACT.Exp)
    act.activation(k.lw, k.lw, ACT.Exp).then_inc(sem.decays_ready, 1)
    act.wait_ge(sem.decays_ready, cnt.next("decays_ready given"))
    for dst in (k.tb, k.tk, k.tv):
        for t in range(2):
            act.wait_ge(sem.act_bank_filled, cnt.next("act_bank"))
            bank = k.bank["act"][(cnt["act_bank"] - 1) % BANKS]
            act.activation(dst[:, t, :], bank, ACT.Copy).then_inc(sem.act_bank_free, 1)


def rwkv_inputs_tensor(pe, cnt, sem, k, l):
    pe.wait_ge(sem.lora_in_ready, cnt.next("lora_in_ready"))
    pe.wait_ge(sem.lora_loaded, 48 * (l + 1))
    for w, rows, x in ((k.lora[:, 0, :], slice(0, 64), ZWA), (k.lora[:, 0, :], slice(64, 128), ZWA),
                       (k.lora[:, 1, :], slice(0, 128), ZG)):
        for c in range(4):
            pe.wait_ge(sem.act_bank_free, cnt["act_bank"] + 1)
            bank = k.bank["act"][cnt["act_bank"] % BANKS]
            pe.matmul(bank[:, 0:SEQ], w[rows, c * P:(c + 1) * P], k.p2[rows, x, :],
                                       start=True, stop=True).then_inc(sem.act_bank_filled, 1)
            cnt.next("act_bank")
    group_norm_tensor(pe, cnt, sem, k, k.ra, 4, SEQ, k.c2["block"])
    pe.wait_ge(sem.bonus_ready, cnt.next("bonus_ready"))
    for c in range(4):
        pe.wait_ge(sem.dve_bank_free, cnt["dve_bank"] + 1)
        bank = k.bank["dve"][cnt["dve_bank"] % BANKS]
        pe.matmul(bank[:, 0:SEQ], k.c2["block"], k.ra[:, c, :], start=True, stop=True).then_inc(sem.dve_bank_filled, 1)
        cnt.next("dve_bank")
    project2_tensor(pe, cnt, sem, k, DECAY_STEPS)
    pe.wait_ge(sem.factors_ready, cnt.next("factors_ready"))
    for src in (k.bi, k.p2[:, ZK:ZK + 4, :], k.p2[:, ZV:ZV + 4, :]):
        for t in range(2):
            pe.wait_ge(sem.act_bank_free, cnt["act_bank"] + 1)
            bank = k.bank["act"][cnt["act_bank"] % BANKS]
            for c in range(4):
                ins = pe.transpose(bank[:, c * P:(c + 1) * P], src[:, c, t * P:(t + 1) * P], k.ident)
            ins.then_inc(sem.act_bank_filled, 1)
            cnt.next("act_bank")
    pe.wait_ge(sem.act_bank_free, BANKS + cnt["act_bank"])


def rwkv_solve_tensor(pe, cnt, sem, k):
    next_step = SOLVE_STEPS[0]
    kz, r = k.p2[:, ZK:ZK + 4, :], k.p2[:, ZR:ZR + 4, :]

    def heads(out_of):
        pe.wait_ge(sem.dve_bank_free, cnt["dve_bank"] + 1)
        bank = k.bank["dve"][cnt["dve_bank"] % BANKS]
        for i in range(4):
            a, b = out_of(i)
            ins = pe.matmul(bank[:, i * P:(i + 1) * P], a, b, start=True, stop=True)
        ins.then_inc(sem.dve_bank_filled, 1)
        cnt.next("dve_bank")

    for t in range(2):
        ts = slice(t * P, (t + 1) * P)
        for p in range(2):
            rows = slice(p * 64, p * 64 + 64)
            for a, b in ((k.ap, k.bi), (k.bi, k.ap), (kz, k.ap), (k.bi, r), (kz, r)):
                heads(lambda i: (a[rows, i, ts], b[rows, i, ts]))
        for phase in range(12):
            for p in range(2):
                x, tri_m, tri_b, tri_n, tri_t = (k.xf[:, p], k.tri_m[p], k.tri_b[p], k.tri_n[p], k.tri_t[p])
                until = SOLVE_STEPS[0] + (SOLVE_STEPS[1] - SOLVE_STEPS[0]) * (24 * t + 2 * phase + p + 1) // 48
                project2_tensor(pe, cnt, sem, k, (next_step, until))
                next_step = until
                pe.wait_ge(sem.tri_ready, cnt.next("tri_ready"))
                if phase < 6 and phase % 2 == 0:
                    heads(lambda i: (tri_b[:, i], tri_m[:, i]))
                    heads(lambda i: (tri_m[:, i], tri_b[:, i]))
                elif phase < 6:
                    heads(lambda i: (tri_m[:, i], x[:, i]))
                    heads(lambda i: (tri_b[:, i], tri_n[:, i]))
                elif phase % 2 == 0:
                    heads(lambda i: (tri_m[:, i], x[:, i]))
                else:
                    heads(lambda i: (tri_n[:, i], tri_t[:, i]))
                    if phase < 11:
                        heads(lambda i: (tri_t[:, i], tri_n[:, i]))
        pe.wait_ge(sem.state_in_ready, cnt.next("state_in_ready"))
        pe.wait_ge(sem.dve_bank_free, cnt["dve_bank"] + 1)
        bank = k.bank["dve"][cnt["dve_bank"] % BANKS]
        for i in range(4):
            cs = slice(i * P, (i + 1) * P)
            pe.matmul(bank[:, cs], k.ap[:, i, ts], k.st[:, i, :], start=True, stop=False)
            for p in range(2):
                hs = slice(i * P + p * 64, i * P + p * 64 + 64)
                ins = pe.matmul(bank[:, hs], k.aak[:, p, i, :], k.tv[:, t, hs], start=False, stop=(p == 1))
        ins.then_inc(sem.dve_bank_filled, 1)
        cnt.next("dve_bank")
        pe.wait_ge(sem.rhs_ready, cnt.next("rhs_ready"))
        pe.wait_ge(sem.dve_bank_free, cnt["dve_bank"] + 1)
        bank = k.bank["dve"][cnt["dve_bank"] % BANKS]
        for i in range(4):
            for p in range(2):
                hs = slice(i * P + p * 64, i * P + p * 64 + 64)
                ins = pe.matmul(bank[:, hs], k.xf[:, p, i, :], k.rhs[:, hs], start=True, stop=True)
        ins.then_inc(sem.dve_bank_filled, 1)
        cnt.next("dve_bank")
        pe.wait_ge(sem.sa_ready, cnt.next("sa_ready"))
        pe.wait_ge(sem.dve_bank_free, cnt["dve_bank"] + 1)
        bank = k.bank["dve"][cnt["dve_bank"] % BANKS]
        for i in range(4):
            cs = slice(i * P, (i + 1) * P)
            pe.matmul(bank[:, cs], k.st[:, i, :], r[:, i, ts], start=True, stop=False, skip_group_check=True)
            for p in range(2):
                hs = slice(i * P + p * 64, i * P + p * 64 + 64)
                rows = slice(p * 64, p * 64 + 64)
                pe.matmul(bank[rows, cs], k.sa[:, hs], k.arb[:, p, i, :], start=False, stop=False,
                            skip_group_check=True)
                ins = pe.matmul(bank[rows, cs], k.tv[:, t, hs], k.ark[:, p, i, :], start=False, stop=True,
                                  skip_group_check=True)
        ins.then_inc(sem.dve_bank_filled, 1)
        cnt.next("dve_bank")
        pe.wait_ge(sem.dve_bank_free, cnt["dve_bank"] + 1)
        bank = k.bank["dve"][cnt["dve_bank"] % BANKS]
        for i in range(4):
            cs = slice(i * P, (i + 1) * P)
            pe.matmul(bank[:, cs], k.tb[:, t, cs], k.sa[:, cs], start=True, stop=False)
            ins = pe.matmul(bank[:, cs], k.tk[:, t, cs], k.tv[:, t, cs], start=False, stop=True)
        ins.then_inc(sem.dve_bank_filled, 1)
        cnt.next("dve_bank")
    pe.wait_ge(sem.y_ready, cnt.next("y_ready"))
    for c in range(4):
        pe.wait_ge(sem.dve_bank_free, cnt["dve_bank"] + 1)
        bank = k.bank["dve"][cnt["dve_bank"] % BANKS]
        pe.matmul(bank[:, 0:SEQ], k.c2["block"], k.lw[:, c, :], start=True, stop=True).then_inc(sem.dve_bank_filled, 1)
        cnt.next("dve_bank")
    group_norm_tensor(pe, cnt, sem, k, k.ra, 4, SEQ, k.c2["block"])


def rwkv_solve_vector(dve, cnt, sem, k, l):
    four = lambda ap: ap.rearrange("p (i n) -> p i n", i=4)
    mask = lambda n: k.c2[n].unsqueeze(1).to_broadcast([P, 4, P])

    def add_bank(dst):
        dve.wait_ge(sem.dve_bank_filled, cnt.next("dve_bank"))
        bank = k.bank["dve"][(cnt["dve_bank"] - 1) % BANKS]
        dve.tensor_tensor(dst, four(bank), dst, ALU.add).then_inc(sem.dve_bank_free, 1)

    def copy_bank(dst):
        dve.wait_ge(sem.dve_bank_filled, cnt.next("dve_bank"))
        bank = k.bank["dve"][(cnt["dve_bank"] - 1) % BANKS]
        dve.tensor_copy(dst, four(bank)).then_inc(sem.dve_bank_free, 1)

    dve.memset(k.st, 0.0).then_inc(sem.dve_done, 1)
    dve.wait_ge(sem.dve_done, cnt.next("dve_done"))
    for t in range(2):
        for p in range(2):
            dve.wait_ge(sem.dve_bank_filled, cnt.next("dve_bank"))
            bank = k.bank["dve"][(cnt["dve_bank"] - 1) % BANKS]
            dve.tensor_copy(k.tri_raw[p], four(bank))
            dve.tensor_tensor(k.tri_m[p], four(bank), mask("low16"), ALU.mult).then_inc(sem.dve_bank_free, 1)
            for dst, name in ((k.tri_b[p], "up16"), (k.aak[:, p], "upper"), (k.arb[:, p], "upper_inc"),
                              (k.ark[:, p], "upper_inc")):
                dve.wait_ge(sem.dve_bank_filled, cnt.next("dve_bank"))
                bank = k.bank["dve"][(cnt["dve_bank"] - 1) % BANKS]
                dve.tensor_tensor(dst, four(bank), mask(name), ALU.mult).then_inc(sem.dve_bank_free, 1)
            dve.wait_ge(sem.dve_bank_free, BANKS + cnt["dve_bank"])
            dve.tensor_tensor(k.xf[:, p], k.tri_b[p], mask("ident"), ALU.add)
            dve.tensor_tensor(k.tri_n[p], k.tri_m[p], mask("ident"), ALU.add).then_inc(sem.tri_ready, 1)
            dve.wait_ge(sem.tri_ready, cnt.next("tri_ready given"))
        for phase in range(12):
            for p in range(2):
                if phase < 6 and phase % 2 == 0:
                    dve.wait_ge(sem.dve_bank_filled, cnt["dve_bank"] + 2)
                    copy_bank(k.tri_m[p])
                    copy_bank(k.tri_b[p])
                elif phase >= 6 and phase % 2 == 0:
                    copy_bank(k.tri_t[p])
                elif phase < 11:
                    dve.wait_ge(sem.dve_bank_filled, cnt["dve_bank"] + 2)
                    add_bank(k.xf[:, p])
                    add_bank(k.tri_n[p])
                    if phase in (5, 7, 9):
                        name = ("low32", "low64", "low128")[(phase - 5) // 2]
                        dve.tensor_tensor(k.tri_m[p], k.tri_raw[p], mask(name), ALU.mult).then_inc(sem.dve_done, 1)
                        dve.wait_ge(sem.dve_done, cnt.next("dve_done"))
                else:
                    add_bank(k.xf[:, p])
                dve.wait_ge(sem.dve_bank_free, BANKS + cnt["dve_bank"])
                if phase < 11:
                    dve.nop().then_inc(sem.tri_ready, 1)
                    cnt.next("tri_ready given")
        mid_exp = k.small[:, 8:16].rearrange("p (c t) -> p c t", c=4)[:, :, t]
        end_exp = k.small[:, 16:24].rearrange("p (c t) -> p c t", c=4)[:, :, t]
        dve.tensor_tensor(k.st, k.st, wide(mid_exp, 4, P), ALU.mult).then_inc(sem.state_in_ready, 1)
        dve.wait_ge(sem.state_in_ready, cnt.next("state_in_ready given"))
        dve.wait_ge(sem.dve_bank_filled, cnt.next("dve_bank"))
        bank = k.bank["dve"][(cnt["dve_bank"] - 1) % BANKS]
        dve.tensor_copy(k.rhs, bank).then_inc(sem.dve_bank_free, 1)
        dve.wait_ge(sem.dve_bank_free, BANKS + cnt["dve_bank"])
        dve.nop().then_inc(sem.rhs_ready, 1)
        cnt.next("rhs_ready given")
        dve.wait_ge(sem.dve_bank_filled, cnt.next("dve_bank"))
        bank = k.bank["dve"][(cnt["dve_bank"] - 1) % BANKS]
        dve.tensor_copy(k.sa, bank).then_inc(sem.dve_bank_free, 1)
        dve.wait_ge(sem.dve_bank_free, BANKS + cnt["dve_bank"])
        dve.nop().then_inc(sem.sa_ready, 1)
        cnt.next("sa_ready given")
        dve.wait_ge(sem.dve_bank_filled, cnt.next("dve_bank"))
        bank = k.bank["dve"][(cnt["dve_bank"] - 1) % BANKS]
        dve.tensor_copy(k.lw[:, :, t * P:(t + 1) * P], four(bank)).then_inc(sem.dve_bank_free, 1)
        dve.wait_ge(sem.dve_bank_filled, cnt.next("dve_bank"))
        bank = k.bank["dve"][(cnt["dve_bank"] - 1) % BANKS]
        dve.tensor_tensor(k.tri_t[0], four(bank), mask("block"), ALU.mult).then_inc(sem.dve_bank_free, 1)
        dve.wait_ge(sem.dve_bank_free, BANKS + cnt["dve_bank"])
        dve.tensor_tensor(k.st, k.st, k.tri_t[0], ALU.add).then_inc(sem.dve_done, 1)
        dve.wait_ge(sem.dve_done, cnt.next("dve_done"))
        dve.tensor_tensor(k.st, k.st, wide(end_exp, 4, P), ALU.mult).then_inc(sem.dve_done, 1)
        dve.wait_ge(sem.dve_done, cnt.next("dve_done"))
    dve.nop().then_inc(sem.y_ready, 1)
    cnt.next("y_ready given")
    for c in range(4):
        dve.wait_ge(sem.dve_bank_filled, cnt.next("dve_bank"))
        bank = k.bank["dve"][(cnt["dve_bank"] - 1) % BANKS]
        y = k.lw[:, c, :]
        dve.scalar_tensor_tensor(y, bank[:, 0:SEQ], -1.0 / 64, y, ALU.mult, ALU.add).then_inc(sem.dve_bank_free, 1)
    dve.wait_ge(sem.dve_bank_free, BANKS + cnt["dve_bank"])
    group_norm_vector(dve, cnt, sem, k, k.lw, k.ra, 4, SEQ, 64, 64e-5)
    dve.tensor_tensor(k.lw, k.lw, wide(k.v2(l, "lnw"), 4, SEQ), ALU.mult).then_inc(sem.dve_done, 1)
    dve.wait_ge(sem.dve_done, cnt.next("dve_done"))
    dve.tensor_tensor(k.lw, k.lw, wide(k.v2(l, "lnb"), 4, SEQ), ALU.add).then_inc(sem.dve_done, 1)
    dve.wait_ge(sem.dve_done, cnt.next("dve_done"))
    dve.tensor_tensor(k.lw, k.lw, k.bonus, ALU.add).then_inc(sem.dve_done, 1)
    dve.wait_ge(sem.dve_done, cnt.next("dve_done"))
    dve.tensor_tensor(k.p2[:, ZR:ZR + 4, :], k.lw, k.g, ALU.mult).then_inc(sem.rwkv_ready, 1)
    dve.wait_ge(sem.rwkv_ready, cnt.next("rwkv_ready given"))


def bias_line_tensor(pe, cnt, sem, k):
    pe.wait_ge(sem.rel_loaded, 16)
    pe.wait_ge(sem.rel_ready, cnt.next("rel_ready"))
    for kind in range(2):
        pe.wait_ge(sem.act_bank_free, cnt["act_bank"] + 1)
        bank = k.bank["act"][cnt["act_bank"] % BANKS]
        pe.matmul(bank[0:8, 0:384], k.rel[0:33, kind * 8:kind * 8 + 8],
                                   k.c2["bucket_full" if kind == 0 else "bucket_win"][0:33, :],
                                   start=True, stop=True).then_inc(sem.act_bank_filled, 1)
        cnt.next("act_bank")


def bias_line_scalar(act, cnt, sem, k):
    for kind in range(2):
        act.wait_ge(sem.act_bank_filled, cnt.next("act_bank"))
        bank = k.bank["act"][(cnt["act_bank"] - 1) % BANKS]
        act.activation(k.line[0:8, kind, :], bank[0:8, 0:384], ACT.Copy).then_inc(sem.act_bank_free, 1)
    act.wait_ge(sem.act_bank_free, BANKS + cnt["act_bank"])
    act.nop().then_inc(sem.line_ready, 1)
    cnt.next("line_ready given")


def nsa_prepare_tensor(pe, cnt, sem, k, l):
    pe.wait_ge(sem.act_bank_free, BANKS + cnt["act_bank"])
    pe.wait_ge(sem.rwkv_ready, cnt.next("rwkv_ready"))
    for kind in range(2):
        pe.wait_ge(sem.bias_loaded, 16 * (2 * l + kind + 1))
        for j in range(4):
            pe.wait_ge(sem.act_bank_free, cnt["act_bank"] + 1)
            bank = k.bank["act"][cnt["act_bank"] % BANKS]
            pe.matmul(bank, k.c2["flip"], k.flipped[:, kind, j * 512:(j + 1) * 512],
                                       start=True, stop=True).then_inc(sem.act_bank_filled, 1)
            cnt.next("act_bank")
    dup = k.c2["dup"].rearrange("p (v n) -> p v n", v=4)
    for src in (KS, KW, SK):
        for g in range(2):
            pe.wait_ge(sem.act_bank_free, cnt["act_bank"] + 1)
            bank = k.bank["act"][cnt["act_bank"] % BANKS]
            for hh in range(2):
                ins = pe.matmul(bank[:, hh * SEQ:(hh + 1) * SEQ], dup[:, g * 2 + hh, :], k.p2[:, src, :],
                                  start=True, stop=True)
            ins.then_inc(sem.act_bank_filled, 1)
            cnt.next("act_bank")
    for srcs in ((VS, VW), (SV,)):
        pe.wait_ge(sem.act_bank_free, cnt["act_bank"] + 1)
        bank = k.bank["act"][cnt["act_bank"] % BANKS]
        n = 0
        for src in srcs:
            for t in range(2):
                ins = pe.transpose(bank[:, n * P:(n + 1) * P], k.p2[:, src, t * P:(t + 1) * P], k.ident)
                n += 1
        ins.then_inc(sem.act_bank_filled, 1)
        cnt.next("act_bank")
    pe.wait_ge(sem.act_bank_free, cnt["act_bank"] + 1)
    bank = k.bank["act"][cnt["act_bank"] % BANKS]
    for t in range(2):
        ins = pe.transpose(bank[:, t * IN_G:(t + 1) * IN_G], k.p2[0:IN_G, NG, t * P:(t + 1) * P],
                             k.ident[0:IN_G, 0:IN_G])
    ins.then_inc(sem.act_bank_filled, 1)
    cnt.next("act_bank")
    pe.wait_ge(sem.pe_loaded, 64 * (l + 1))
    for kind in range(2):
        pe.wait_ge(sem.act_bank_free, cnt["act_bank"] + 1)
        bank = k.bank["act"][cnt["act_bank"] % BANKS]
        pe.transpose(bank[:, 0:32], k.perow[0:32, kind, :], k.ident[0:32, 0:32]).then_inc(sem.act_bank_filled, 1)
        cnt.next("act_bank")
    for kind in range(2):
        pe.wait_ge(sem.blocks_ready, cnt.next("blocks_ready"))
        pe.wait_ge(sem.act_bank_free, cnt["act_bank"] + 1)
        bank = k.bank["act"][cnt["act_bank"] % BANKS]
        for part in range(4):
            pe.wait_ge(sem.panel_loaded[cnt["panel"] % RING], k.panel_value[cnt["panel"]])
            panel = k.panel(cnt.next("panel") - 1, 256)
            for pos in range(8):
                lpos = part * 8 + pos
                half, at = lpos // 16, lpos % 16
                first = half * 2 * SEQ + 16 * half + at
                ins = pe.matmul(bank[0:31, 0:256], k.zzflat[:, first:first + 30 * 16 + 1:16], panel[:, pos, :],
                                  start=(lpos == 0), stop=(lpos == 31))
                if pos == 0:
                    ins.then_inc(sem.panel_used, 1)
        ins.then_inc(sem.act_bank_filled, 1)
        cnt.next("act_bank")
        pe.wait_ge(sem.act_bank_free, BANKS + cnt["act_bank"])
        pe.wait_ge(sem.act_bank_free, cnt["act_bank"] + 1)
        bank = k.bank["act"][cnt["act_bank"] % BANKS]
        for hc in range(2):
            ins = pe.transpose(bank[:, hc * 32:hc * 32 + 31], k.hidrow[0:31, hc * P:(hc + 1) * P],
                                 k.ident[0:31, 0:31])
        ins.then_inc(sem.act_bank_filled, 1)
        cnt.next("act_bank")
        pe.wait_ge(sem.act_bank_free, BANKS + cnt["act_bank"])
        pe.wait_ge(sem.w2_loaded, 16 * (2 * l + kind + 1))
        w2 = k.cw2[:, kind, :, :]
        pe.wait_ge(sem.act_bank_free, cnt["act_bank"] + 1)
        bank = k.bank["act"][cnt["act_bank"] % BANKS]
        if kind == 0:
            for hh in range(2):
                for hc in range(2):
                    ins = pe.matmul(bank[hh * 64:hh * 64 + 64, 0:31], w2[:, hc, :], k.hid[:, hc, 0:31],
                                      start=(hc == 0), stop=(hc == 1))
        else:
            for g in range(2):
                for hc in range(2):
                    ins = pe.matmul(bank[0:15, g * 64:g * 64 + 64], k.hid[:, hc, g * 16:g * 16 + 15], w2[:, hc, :],
                                      start=(hc == 0), stop=(hc == 1))
        ins.then_inc(sem.act_bank_filled, 1)
        cnt.next("act_bank")
    pe.wait_ge(sem.act_bank_free, BANKS + cnt["act_bank"])


def nsa_prepare_scalar(act, cnt, sem, k, l):
    for kind in range(2):
        for j in range(4):
            act.wait_ge(sem.act_bank_filled, cnt.next("act_bank"))
            bank = k.bank["act"][(cnt["act_bank"] - 1) % BANKS]
            act.activation(k.bias[:, kind, 2 * j:2 * j + 2, :], bank.rearrange("p (h n) -> p h n", h=2), ACT.Copy).then_inc(sem.act_bank_free, 1)
    for kind in range(3):
        for g in range(2):
            act.wait_ge(sem.act_bank_filled, cnt.next("act_bank"))
            bank = k.bank["act"][(cnt["act_bank"] - 1) % BANKS]
            act.activation(k.kp[:, kind, 2 * g:2 * g + 2, :], bank.rearrange("p (h n) -> p h n", h=2), ACT.Copy).then_inc(sem.act_bank_free, 1)
    for a, n in ((0, 2), (2, 1)):
        act.wait_ge(sem.act_bank_filled, cnt.next("act_bank"))
        bank = k.bank["act"][(cnt["act_bank"] - 1) % BANKS]
        act.activation(k.vtt[:, a:a + n, :, :], bank[:, 0:n * 256].rearrange("p (s t n) -> p s t n", s=n, t=2), ACT.Copy).then_inc(sem.act_bank_free, 1)
    act.wait_ge(sem.act_bank_filled, cnt.next("act_bank"))
    bank = k.bank["act"][(cnt["act_bank"] - 1) % BANKS]
    act.activation(k.gt, bank[:, 0:48].rearrange("p (t n) -> p t n", t=2), ACT.Copy).then_inc(sem.act_bank_free, 1)
    for kind in range(2):
        act.wait_ge(sem.act_bank_filled, cnt.next("act_bank"))
        bank = k.bank["act"][(cnt["act_bank"] - 1) % BANKS]
        act.activation(k.pecol[:, kind, :], bank[:, 0:32], ACT.Copy).then_inc(sem.act_bank_free, 1)
    act.wait_ge(sem.act_bank_free, BANKS + cnt["act_bank"])
    act.nop().then_inc(sem.pecol_ready, 1)
    cnt.next("pecol_ready given")
    act.wait_ge(sem.blocks_zeroed, cnt.next("blocks_zeroed"))
    for kind in range(2):
        act.wait_ge(sem.act_bank_filled, cnt.next("act_bank"))
        bank = k.bank["act"][(cnt["act_bank"] - 1) % BANKS]
        act.activation(k.hidrow[0:31, :], bank[0:31, 0:256], ACT.Gelu).then_inc(sem.act_bank_free, 1)
        if kind == 0:
            act.wait_ge(sem.act_bank_free, BANKS + cnt["act_bank"])
            act.nop().then_inc(sem.hidden_read, 1)
            cnt.next("hidden_read given")
        act.wait_ge(sem.act_bank_filled, cnt.next("act_bank"))
        bank = k.bank["act"][(cnt["act_bank"] - 1) % BANKS]
        act.activation(k.hid[:, :, 0:31],
                                            bank[:, 0:64].rearrange("p (c n) -> p c n", c=2)[:, :, 0:31], ACT.Copy).then_inc(sem.act_bank_free, 1)
        act.wait_ge(sem.act_bank_filled, cnt.next("act_bank"))
        bank = k.bank["act"][(cnt["act_bank"] - 1) % BANKS]
        if kind == 0:
            blocks = bank[:, 0:32].rearrange("p (g n) -> p g n", g=2)[:, :, 0:15]
            act.activation(k.kcp[0:64, :, 0, 0:15], blocks[0:64], ACT.Copy)
            act.activation(k.kcp[64:128, :, 1, 0:15], blocks[64:128], ACT.Copy).then_inc(sem.act_bank_free, 1)
        else:
            act.activation(k.vcp[0:15, :], bank[0:15, 0:128], ACT.Copy).then_inc(sem.act_bank_free, 1)
    act.wait_ge(sem.act_bank_free, BANKS + cnt["act_bank"])
    act.nop().then_inc(sem.nsa_keys_ready, 1)
    cnt.next("nsa_keys_ready given")


def nsa_prepare_vector(dve, cnt, sem, k, l):
    dve.memset(k.zz, 0.0)
    dve.memset(k.kcp, 0.0)
    dve.memset(k.vcp, 0.0)
    dve.memset(k.ew, 0.0)
    dve.tensor_scalar(k.cmadd, k.c2["cmp_mask"], -1.0, -NEG, ALU.add, ALU.mult).then_inc(sem.blocks_zeroed, 1)
    dve.wait_ge(sem.blocks_zeroed, cnt.next("blocks_zeroed given"))
    dve.wait_ge(sem.pecol_ready, cnt.next("pecol_ready"))
    for kind, src in enumerate((KC, VC)):
        if kind == 1:
            dve.wait_ge(sem.hidden_read, cnt.next("hidden_read"))
        for g in range(2):
            rows = slice(g * 64, g * 64 + 64)
            z = k.p2[rows, src, :].rearrange("p (n l) -> p n l", l=16)
            for half in range(2):
                pe = k.pecol[rows, kind, half * 16:half * 16 + 16].unsqueeze(1).to_broadcast([64, 16, 16])
                ins = dve.tensor_tensor(k.zz[rows, half, g, :].rearrange("p (n l) -> p n l", l=16), z, pe, ALU.add)
        ins.then_inc(sem.blocks_ready, 1)
        dve.wait_ge(sem.blocks_ready, cnt.next("blocks_ready given"))


def att2_items():
    return [(h, q) for h in range(8) for q in range(2)]


SEL0, WIN0, SWA0 = 128, 384, 640


def attention2_tensor(pe, cnt, sem, k, l):
    items = att2_items()

    def scores(i):
        h, q = items[i]
        n, g, hh = (q + 1) * P, h // 4, h % 2
        qs = slice(q * P, (q + 1) * P)
        pe.wait_ge(sem.dve_bank_free, cnt["dve_bank"] + 1)
        bank = k.bank["dve"][cnt["dve_bank"] % BANKS]
        for kind in range(2):
            ins = pe.matmul(bank[:, kind * 256:kind * 256 + n], k.p2[:, NQ + h // 2, qs],
                              k.kp[:, kind, 2 * g + hh, 0:n], start=True, stop=True)
        ins.then_inc(sem.dve_bank_filled, 1)
        cnt.next("dve_bank")
        pe.wait_ge(sem.dve_bank_free, cnt["dve_bank"] + 1)
        bank = k.bank["dve"][cnt["dve_bank"] % BANKS]
        pe.matmul(bank[:, 0:16], k.p2[:, NQ + h // 2, qs], k.kcp[:, g, hh, :], start=True, stop=True)
        pe.matmul(bank[:, 256:256 + n], k.p2[:, SQ + h // 2, qs], k.kp[:, 2, 2 * g + hh, 0:n],
                                   start=True, stop=True).then_inc(sem.dve_bank_filled, 1)
        cnt.next("dve_bank")

    def transposes(i):
        blocks = blocks_of(items[i][1])
        pe.wait_ge(sem.weights_ready, cnt.next("weights_ready"))
        for b0 in (0, 4):
            part = blocks[b0:b0 + 4]
            if not part:
                continue
            pe.wait_ge(sem.act_bank_free, cnt["act_bank"] + 1)
            bank = k.bank["act"][cnt["act_bank"] % BANKS]
            for j, (col, _, _) in enumerate(part):
                ins = pe.transpose(bank[:, j * P:(j + 1) * P], k.ew[:, i % 3, col:col + P], k.ident)
            ins.then_inc(sem.act_bank_filled, 1)
            cnt.next("act_bank")

    def outputs(i, transposed):
        h, q = items[i]
        g, hh = h // 4, h % 2
        blocks = blocks_of(q)
        pe.wait_ge(sem.act_bank_free, BANKS + transposed)
        pe.wait_ge(sem.act_bank_free, cnt["act_bank"] + 1)
        bank = k.bank["act"][cnt["act_bank"] % BANKS]
        rows = slice(hh * 64, hh * 64 + 64)
        for want, cols in ((False, slice(0, P)), (True, slice(P, 2 * P))):
            mine = [j for j, b in enumerate(blocks) if (b[1] == 2) == want]
            for j in mine:
                _, kind, t = blocks[j]
                v = k.vcp[:, g * 64:g * 64 + 64] if kind is None else k.vtt[:, kind, t, g * 64:g * 64 + 64]
                ins = pe.matmul(bank[rows, cols], v, k.ewt[:, i % 2, j, :], start=(j == mine[0]), stop=(j == mine[-1]))
        ins.then_inc(sem.act_bank_filled, 1)
        cnt.next("act_bank")

    scores(0)
    scores(1)
    transposed = 0
    for i in range(len(items)):
        if i + 2 < len(items):
            scores(i + 2)
        transposes(i)
        before, transposed = transposed, cnt["act_bank"]
        if i > 0:
            outputs(i - 1, before)
        done = ATTENTION_STEPS[0] + i // 4 * 2 + i % 4
        if i % 4 < 2:
            project2_tensor(pe, cnt, sem, k, (done, done + 1))
        else:
            branch_step_tensor(pe, cnt, sem, k, ZR, i // 4 * 2 + i % 4 - 2)
    outputs(len(items) - 1, transposed)
    pe.wait_ge(sem.act_bank_free, BANKS + cnt["act_bank"])


def blocks_of(q):
    out = [(0, None, 0)]
    for kind, col in ((0, SEL0), (1, WIN0), (2, SWA0)):
        out += [(col + t * P, kind, t) for t in range(q + 1)]
    return out


def attention2_scalar(act, cnt, sem, k, l):
    items = att2_items()

    def exponentials(i):
        h, q = items[i]
        n = (q + 1) * P
        act.wait_ge(sem.neg_max_ready, cnt.next("neg_max_ready"))
        s = k.stat2[:, i % 3, :]
        for j, (col, width) in enumerate(((0, 16), (SEL0, n), (WIN0, n), (SWA0, n))):
            w = k.ew[:, i % 3, col:col + width]
            act.activation(w, w, ACT.Exp, bias=s[:, j:j + 1], accum_out=s[:, 4 + j:5 + j])
        act.activation(s[:, 8:9], k.sinks[:, h:h + 1], ACT.Exp, bias=s[:, 3:4]).then_inc(sem.exp_ready, 1)
        act.wait_ge(sem.exp_ready, cnt.next("exp_ready given"))

    def outputs(i):
        h, q = items[i]
        act.wait_ge(sem.act_bank_filled, cnt.next("act_bank"))
        bank = k.bank["act"][(cnt["act_bank"] - 1) % BANKS]
        rows = slice((h % 2) * 64, (h % 2) * 64 + 64)
        act.activation(k.p2[rows, ZK + h // 2, q * P:(q + 1) * P], bank[rows, 0:P], ACT.Copy)
        act.activation(k.p2[rows, ZV + h // 2, q * P:(q + 1) * P], bank[rows, P:2 * P], ACT.Copy).then_inc(sem.act_bank_free, 1)

    exponentials(0)
    exponentials(1)
    for i, (h, q) in enumerate(items):
        blocks = blocks_of(q)
        for b0 in (0, 4):
            m = len(blocks[b0:b0 + 4])
            if not m:
                continue
            act.wait_ge(sem.act_bank_filled, cnt.next("act_bank"))
            bank = k.bank["act"][(cnt["act_bank"] - 1) % BANKS]
            act.activation(k.ewt[:, i % 2, b0:b0 + m, :],
                                                bank[:, 0:m * P].rearrange("p (b n) -> p b n", n=P), ACT.Copy).then_inc(sem.act_bank_free, 1)
        if i + 2 < len(items):
            exponentials(i + 2)
        if i > 0:
            outputs(i - 1)
        if i % 4 < 2:
            done = ATTENTION_STEPS[0] + i // 4 * 2 + i % 4
            project2_scalar(act, cnt, sem, k, (done, done + 1))
    outputs(len(items) - 1)
    act.wait_ge(sem.act_bank_free, BANKS + cnt["act_bank"])
    act.nop().then_inc(sem.attention2_ready, 1)
    cnt.next("attention2_ready given")


def attention2_vector(dve, cnt, sem, k, l):
    items = att2_items()
    dve.wait_ge(sem.nsa_keys_ready, cnt.next("nsa_keys_ready"))
    dve.wait_ge(sem.sinks_loaded, 16 * (l + 1))
    scale = 64 ** -0.5

    def maxima(i):
        h, q = items[i]
        s, w = k.stat2[:, i % 3, :], k.ew[:, i % 3, :]
        n = (q + 1) * P
        j0 = P * (1 - q)
        dve.wait_ge(sem.dve_bank_filled, cnt.next("dve_bank"))
        bank = k.bank["dve"][(cnt["dve_bank"] - 1) % BANKS]
        both = w[:, SEL0:SEL0 + 512].rearrange("p (b n) -> p b n", b=2)[:, :, 0:n]
        bias = k.bias[:, 0, h, j0:j0 + n].unsqueeze(1).to_broadcast([P, 2, n])
        dve.scalar_tensor_tensor(both, bank.rearrange("p (b n) -> p b n", b=2)[:, :, 0:n], scale,
                                                      bias, ALU.mult, ALU.add).then_inc(sem.dve_bank_free, 1)
        dve.wait_ge(sem.dve_bank_filled, cnt.next("dve_bank"))
        bank = k.bank["dve"][(cnt["dve_bank"] - 1) % BANKS]
        dve.scalar_tensor_tensor(w[:, 0:16], bank[:, 0:16], scale, k.cmadd[:, q * 16:q * 16 + 16], ALU.mult, ALU.add)
        dve.scalar_tensor_tensor(w[:, SWA0:SWA0 + n], bank[:, 256:256 + n], scale,
                                                      k.bias[:, 1, h, j0:j0 + n], ALU.mult, ALU.add).then_inc(sem.dve_bank_free, 1)
        dve.wait_ge(sem.dve_bank_free, BANKS + cnt["dve_bank"])
        dve.tensor_reduce(s[:, 0:1], w[:, 0:16], AX, ALU.max)
        dve.tensor_reduce(s[:, 1:3], both, AX, ALU.max)
        dve.tensor_reduce(s[:, 3:4], w[:, SWA0:SWA0 + n], AX, ALU.max).then_inc(sem.dve_done, 1)
        dve.wait_ge(sem.dve_done, cnt.next("dve_done"))
        dve.tensor_tensor(s[:, 3:4], s[:, 3:4], k.sinks[:, h:h + 1], ALU.max).then_inc(sem.dve_done, 1)
        dve.wait_ge(sem.dve_done, cnt.next("dve_done"))
        dve.tensor_scalar(s[:, 0:4], s[:, 0:4], -1.0, None, ALU.mult).then_inc(sem.neg_max_ready, 1)
        dve.wait_ge(sem.neg_max_ready, cnt.next("neg_max_ready given"))

    maxima(0)
    maxima(1)
    for i, (h, q) in enumerate(items):
        s, w = k.stat2[:, i % 3, :], k.ew[:, i % 3, :]
        n = (q + 1) * P
        dve.wait_ge(sem.exp_ready, cnt.next("exp_ready"))
        dve.tensor_tensor(w[:, 0:16], w[:, 0:16], k.c2["cmp_mask"][:, q * 16:q * 16 + 16], ALU.mult).then_inc(sem.dve_done, 1)
        dve.wait_ge(sem.dve_done, cnt.next("dve_done"))
        dve.tensor_reduce(s[:, 4:5], w[:, 0:16], AX, ALU.add).then_inc(sem.dve_done, 1)
        dve.wait_ge(sem.dve_done, cnt.next("dve_done"))
        dve.tensor_tensor(s[:, 7:8], s[:, 7:8], s[:, 8:9], ALU.add).then_inc(sem.dve_done, 1)
        dve.wait_ge(sem.dve_done, cnt.next("dve_done"))
        dve.tensor_scalar(s[:, 4:7], s[:, 4:7], 1e-30, None, ALU.max).then_inc(sem.dve_done, 1)
        dve.wait_ge(sem.dve_done, cnt.next("dve_done"))
        dve.reciprocal(s[:, 4:8], s[:, 4:8]).then_inc(sem.dve_done, 1)
        dve.wait_ge(sem.dve_done, cnt.next("dve_done"))
        dve.tensor_tensor(s[:, 4:7], s[:, 4:7], k.gt[:, q, h * 3:h * 3 + 3], ALU.mult).then_inc(sem.dve_done, 1)
        dve.wait_ge(sem.dve_done, cnt.next("dve_done"))
        for j, (col, width) in enumerate(((0, 16), (SEL0, n), (WIN0, n), (SWA0, n))):
            ins = dve.tensor_scalar(w[:, col:col + width], w[:, col:col + width], s[:, 4 + j:5 + j], None, ALU.mult)
        ins.then_inc(sem.weights_ready, 1)
        dve.wait_ge(sem.weights_ready, cnt.next("weights_ready given"))
        if i + 2 < len(items):
            maxima(i + 2)
        if i % 4 >= 2:
            gate = k.p2[:, GATES + i // 4 * 2 + i % 4 - 2, :]
            dve.wait_ge(sem.dve_bank_filled, cnt.next("dve_bank"))
            bank = k.bank["dve"][(cnt["dve_bank"] - 1) % BANKS]
            dve.tensor_tensor(gate, bank[:, 0:SEQ], gate, ALU.mult).then_inc(sem.dve_bank_free, 1)


def branch_step_tensor(pe, cnt, sem, k, src, c):
    if c % 2 == 0:
        pe.wait_ge(sem.panel_loaded[cnt["panel"] % RING], k.panel_value[cnt["panel"]])
        cnt.next("panel")
    panel = k.panel(cnt["panel"] - 1)
    m = c % 2
    pe.wait_ge(sem.dve_bank_free, cnt["dve_bank"] + 1)
    bank = k.bank["dve"][cnt["dve_bank"] % BANKS]
    for kc in range(4):
        ins = pe.matmul(bank[:, 0:SEQ], panel[:, kc, m * P:(m + 1) * P], k.p2[:, src + kc, :],
                          start=(kc == 0), stop=(kc == 3))
        if m == 0 and kc == 0:
            ins.then_inc(sem.panel_used, 1)
    ins.then_inc(sem.dve_bank_filled, 1)
    cnt.next("dve_bank")


def branches_tensor(pe, cnt, sem, k, l):
    for src in (ZK, ZV):
        for c in range(DC):
            branch_step_tensor(pe, cnt, sem, k, src, c)
    pe.wait_ge(sem.merged_ready, cnt.next("merged_ready"))
    for j in range(4):
        pe.wait_ge(sem.panel_loaded[cnt["panel"] % RING], k.panel_value[cnt["panel"]])
        panel = k.panel(cnt.next("panel") - 1)
        for m in range(2):
            pe.wait_ge(sem.dve_bank_free, cnt["dve_bank"] + 1)
            bank = k.bank["dve"][cnt["dve_bank"] % BANKS]
            for kc in range(DC):
                ins = pe.matmul(bank[:, 0:SEQ], panel[:, kc, m * P:(m + 1) * P], k.merged[:, kc, :],
                                  start=(kc == 0), stop=(kc == 7))
                if m == 0 and kc == 0:
                    ins.then_inc(sem.panel_used, 1)
            ins.then_inc(sem.dve_bank_filled, 1)
            cnt.next("dve_bank")


def branches_vector(dve, cnt, sem, k, l):
    dve.wait_ge(sem.attention2_ready, cnt.next("attention2_ready"))
    for b in (1, 2):
        for c in range(DC):
            dve.wait_ge(sem.dve_bank_filled, cnt.next("dve_bank"))
            bank = k.bank["dve"][(cnt["dve_bank"] - 1) % BANKS]
            gate = k.p2[:, GATES + b * DC + c, :]
            before = k.p2[:, GATES + c, :] if b == 1 else k.merged[:, c, :]
            t = k.btmp[:, c % 2, :]
            dve.tensor_tensor(t, bank[:, 0:SEQ], gate, ALU.mult).then_inc(sem.dve_bank_free, 1)
            dve.wait_ge(sem.dve_bank_free, BANKS + cnt["dve_bank"])
            dve.tensor_tensor(k.merged[:, c, :], before, t, ALU.add).then_inc(sem.dve_done, 1)
            dve.wait_ge(sem.dve_done, cnt.next("dve_done"))
    dve.nop().then_inc(sem.merged_ready, 1)
    cnt.next("merged_ready given")
    for c in range(DC):
        dve.wait_ge(sem.dve_bank_filled, cnt.next("dve_bank"))
        bank = k.bank["dve"][(cnt["dve_bank"] - 1) % BANKS]
        dve.tensor_tensor(k.x2[:, c, :], bank[:, 0:SEQ], k.x2[:, c, :], ALU.add).then_inc(sem.dve_bank_free, 1)
    dve.wait_ge(sem.dve_bank_free, BANKS + cnt["dve_bank"])


def peer_tensor(pe, cnt, sem, k, l):
    pe.wait_ge(sem.panel_loaded[cnt["panel"] % RING], k.panel_value[cnt["panel"]])
    panel = k.panel(cnt.next("panel") - 1, P)
    for j in range(4):
        pe.wait_ge(sem.act_bank_free, cnt["act_bank"] + 1)
        bank = k.bank["act"][cnt["act_bank"] % BANKS]
        for m in range(4):
            ins = pe.transpose(bank[:, m * P:(m + 1) * P], panel[:, 4 * j + m, :], k.ident)
            if m == 0 and j == 0:
                ins.then_inc(sem.panel_used, 1)
        ins.then_inc(sem.act_bank_filled, 1)
        cnt.next("act_bank")
    for j in range(PEER_H + 1):
        if j < PEER_H:
            pe.wait_ge(sem.panel_loaded[cnt["panel"] % RING], k.panel_value[cnt["panel"]])
            panel = k.panel(cnt.next("panel") - 1)
            for m in range(2):
                pe.wait_ge(sem.act_bank_free, cnt["act_bank"] + 1)
                bank = k.bank["act"][cnt["act_bank"] % BANKS]
                for kc in range(DC):
                    if j == 0 and m == 0:
                        pe.wait_ge(sem.xn_ready, cnt.next("xn_ready"))
                    ins = pe.matmul(bank[:, 0:SEQ], panel[:, kc, m * P:(m + 1) * P], k.xn2[:, kc, :],
                                      start=(kc == 0), stop=(kc == 7))
                    if m == 0 and kc == 0:
                        ins.then_inc(sem.panel_used, 1)
                ins.then_inc(sem.act_bank_filled, 1)
                cnt.next("act_bank")
        if j > 0:
            pe.wait_ge(sem.act_bank_free, BANKS + cnt["act_bank"] - (2 if j < PEER_H else 0))
            pe.wait_ge(sem.act_bank_free, cnt["act_bank"] + 1)
            bank = k.bank["act"][cnt["act_bank"] % BANKS]
            for t in range(2):
                for m in range(2):
                    r = 2 * (j - 1) + m
                    at = (2 * t + m) * P
                    ins = pe.matmul(bank[:, at:at + P], k.pq[:, r, t * P:(t + 1) * P], k.skt[:, r, :],
                                      start=True, stop=True)
            ins.then_inc(sem.act_bank_filled, 1)
            cnt.next("act_bank")
    store_features_tensor(pe, cnt, sem, k, k.xn2)
    pe.wait_ge(sem.experts_summed, cnt.next("experts_summed"))
    for j in range(4):
        pe.wait_ge(sem.dve_bank_free, cnt["dve_bank"] + 1)
        bank = k.bank["dve"][cnt["dve_bank"] % BANKS]
        for m in range(2):
            for t in range(2):
                c = 2 * j + m
                ins = pe.transpose(bank[:, m * SEQ + t * P:m * SEQ + (t + 1) * P], k.acc[:, t, c * P:(c + 1) * P],
                                     k.ident)
        ins.then_inc(sem.dve_bank_filled, 1)
        cnt.next("dve_bank")


def peer_scalar(act, cnt, sem, k, l):
    for j in range(4):
        act.wait_ge(sem.act_bank_filled, cnt.next("act_bank"))
        bank = k.bank["act"][(cnt["act_bank"] - 1) % BANKS]
        act.activation(k.skt[:, 4 * j:4 * j + 4, :], bank.rearrange("p (m n) -> p m n", m=4),
                                            ACT.Copy).then_inc(sem.act_bank_free, 1)
    for j in range(PEER_H + 1):
        if j < PEER_H:
            for m in range(2):
                act.wait_ge(sem.act_bank_filled, cnt.next("act_bank"))
                bank = k.bank["act"][(cnt["act_bank"] - 1) % BANKS]
                act.activation(k.pq[:, 2 * j + m, :], bank[:, 0:SEQ], ACT.Copy).then_inc(sem.act_bank_free, 1)
        if j > 0:
            act.wait_ge(sem.act_bank_filled, cnt.next("act_bank"))
            bank = k.bank["act"][(cnt["act_bank"] - 1) % BANKS]
            act.activation(k.ps[:, :, 2 * j - 2:2 * j, :],
                                                bank.rearrange("p (t m n) -> p t m n", t=2, m=2), ACT.Copy).then_inc(sem.act_bank_free, 1)
            act.wait_ge(sem.act_bank_free, BANKS + cnt["act_bank"])
            act.nop().then_inc(sem.head_scores_ready, 1)
            cnt.next("head_scores_ready given")
    store_features_scalar(act, cnt, sem, k, k.zt)
    act.nop().then_inc(sem.token_rows_ready, 1)
    cnt.next("token_rows_ready given")
    for t in range(2):
        act.wait_ge(sem.best_ready, cnt.next("best_ready"))
        act.activation(k.gate[:, t], k.gate[:, t], ACT.Exp).then_inc(sem.gate_exp_ready, 1)
        act.wait_ge(sem.gate_exp_ready, cnt.next("gate_exp_ready given"))
        act.wait_ge(sem.dots_ready, cnt.next("dots_ready"))
        act.activation(k.hdot, k.hdot, ACT.Gelu).then_inc(sem.gelu_ready, 1)
        act.wait_ge(sem.gelu_ready, cnt.next("gelu_ready given"))


def top16(dve, cnt, sem, k, values, index, scores):
    dve.max(values[:, 0:8], scores).then_inc(sem.dve_done, 1)
    dve.wait_ge(sem.dve_done, cnt.next("dve_done"))
    dve.max_index(index[:, 0:8], values[:, 0:8], scores)
    dve.match_replace(scores, values[:, 0:8], scores, -3.0e38).then_inc(sem.dve_done, 1)
    dve.wait_ge(sem.dve_done, cnt.next("dve_done"))
    dve.max(values[:, 8:16], scores).then_inc(sem.dve_done, 1)
    dve.wait_ge(sem.dve_done, cnt.next("dve_done"))
    dve.max_index(index[:, 8:16], values[:, 8:16], scores).then_inc(sem.dve_done, 1)
    dve.wait_ge(sem.dve_done, cnt.next("dve_done"))


def gather_count(l, t, table, j):
    return ((l * 2 + t) * 2 + table) * 128 + j


def rank_step(dve, cnt, sem, k, t, h, step):
    if step < 2:
        r = 2 * h + step
        top16(dve, cnt, sem, k, k.tv16[:, r, :], k.ti16[:, r, :], k.ps[:, t, r, :])
        return
    dve.tensor_copy(k.tif[:, 2 * h:2 * h + 2, :], k.ti16[:, 2 * h:2 * h + 2, :])
    cand = k.cand.rearrange("p (a b) -> p a b", a=16)
    a = k.tv16[:, 2 * h, :].unsqueeze(2).to_broadcast([P, 16, 16])
    b = k.tv16[:, 2 * h + 1, :].unsqueeze(1).to_broadcast([P, 16, 16])
    dve.tensor_tensor(cand, a, b, ALU.add).then_inc(sem.dve_done, 1)
    dve.wait_ge(sem.dve_done, cnt.next("dve_done"))
    top16(dve, cnt, sem, k, k.gate[:, t, h, :], k.flat[:, h, :], k.cand)


def pick_step(dve, cnt, sem, k, l, t, step):
    if step < 2:
        half = step
        if half == 0:
            dve.tensor_scalar(k.rank[:, 0], k.flat, 4, None, ALU.logical_shift_right)
            dve.tensor_scalar(k.rank[:, 1], k.flat, 15, None, ALU.bitwise_and).then_inc(sem.dve_done, 1)
            dve.wait_ge(sem.dve_done, cnt.next("dve_done"))
            dve.tensor_copy(k.rankf, k.rank).then_inc(sem.dve_done, 1)
            dve.wait_ge(sem.dve_done, cnt.next("dve_done"))
        iota = k.c2["iota16"].unsqueeze(1).to_broadcast([P, 128, 16])
        rk = k.rankf[:, half].rearrange("p h k -> p (h k)").unsqueeze(2).to_broadcast([P, 128, 16])
        dve.tensor_tensor(k.hot, rk, iota, ALU.is_equal).then_inc(sem.dve_done, 1)
        dve.wait_ge(sem.dve_done, cnt.next("dve_done"))
        hot = k.hot.rearrange("p (h k) c -> p h k c", h=8)
        keys = k.tif[:, half::2, :]
        for h in range(PEER_H):
            ins = dve.tensor_tensor(hot[:, h], hot[:, h], keys[:, h, :].unsqueeze(1).to_broadcast([P, 16, 16]),
                                      ALU.mult)
        ins.then_inc(sem.dve_done, 1)
        dve.wait_ge(sem.dve_done, cnt.next("dve_done"))
        dve.tensor_reduce(k.key[:, half, :], k.hot, AX, ALU.add).then_inc(sem.dve_done, 1)
        dve.wait_ge(sem.dve_done, cnt.next("dve_done"))
        return
    dve.scalar_tensor_tensor(k.key[:, 0, :], k.key[:, 0, :], float(NKEYS), k.key[:, 1, :], ALU.mult,
                                      ALU.add).then_inc(sem.dve_done, 1)
    dve.wait_ge(sem.dve_done, cnt.next("dve_done"))
    dve.tensor_scalar(k.key[:, 0, :], k.key[:, 0, :], float(l * NKEYS * NKEYS), None, ALU.add).then_inc(sem.dve_done, 1)
    dve.wait_ge(sem.dve_done, cnt.next("dve_done"))
    dve.tensor_copy(k.expert[:, t, :], k.key[:, 0, :]).then_inc(sem.experts_ready, 1)
    dve.wait_ge(sem.experts_ready, cnt.next("experts_ready given"))
    best, gate = k.gmax, k.gate[:, t]
    dve.tensor_copy(best, gate[:, :, 0]).then_inc(sem.dve_done, 1)
    dve.wait_ge(sem.dve_done, cnt.next("dve_done"))
    dve.tensor_tensor(gate, gate, wide(best, 8, 16), ALU.subtract).then_inc(sem.best_ready, 1)
    dve.wait_ge(sem.best_ready, cnt.next("best_ready given"))


def gate_step(dve, cnt, sem, k, t):
    best, gate = k.gmax, k.gate[:, t]
    dve.wait_ge(sem.gate_exp_ready, cnt.next("gate_exp_ready"))
    dve.tensor_reduce(best, gate, AX, ALU.add).then_inc(sem.dve_done, 1)
    dve.wait_ge(sem.dve_done, cnt.next("dve_done"))
    dve.reciprocal(best, best).then_inc(sem.dve_done, 1)
    dve.wait_ge(sem.dve_done, cnt.next("dve_done"))
    dve.tensor_tensor(gate, gate, wide(best, 8, 16), ALU.mult).then_inc(sem.dve_done, 1)
    dve.wait_ge(sem.dve_done, cnt.next("dve_done"))


def peer_vector(dve, cnt, sem, k, l):
    for h in range(PEER_H):
        dve.wait_ge(sem.head_scores_ready, cnt.next("head_scores_ready"))
        for step in range(3):
            rank_step(dve, cnt, sem, k, 0, h, step)
    for step in range(3):
        pick_step(dve, cnt, sem, k, l, 0, step)
    gate_step(dve, cnt, sem, k, 0)
    dve.wait_ge(sem.token_rows_ready, cnt.next("token_rows_ready"))
    slots = len(k.gather)
    for t in range(2):
        for table in range(2):
            for j in range(128):
                row_number = table * 128 + j
                if t == 0 and row_number % 8 == 7:
                    step = row_number // 8
                    if step < 3 * PEER_H:
                        rank_step(dve, cnt, sem, k, 1, step // 3, step % 3)
                    elif step < 3 * PEER_H + 3:
                        pick_step(dve, cnt, sem, k, l, 1, step - 3 * PEER_H)
                    elif step == 3 * PEER_H + 3:
                        gate_step(dve, cnt, sem, k, 1)
                n = gather_count(l, t, table, j)
                dve.wait_ge(sem.row_gathered[n % slots], 16 * (n // slots + 1))
                row = k.gather[n % slots]
                if table == 0:
                    ins = dve.tensor_tensor_reduce(row, row, k.zt[:, t, :], 1.0, 0.0, ALU.mult, ALU.add,
                                                     k.hdot[:, j:j + 1])
                elif j == 0:
                    ins = dve.tensor_scalar(k.acc[:, t, :], row, k.hdot[:, j:j + 1], None, ALU.mult)
                else:
                    dve.wait_ge(sem.row_used, n)
                    ins = dve.scalar_tensor_tensor(k.acc[:, t, :], row, k.hdot[:, j:j + 1], k.acc[:, t, :],
                                                     ALU.mult, ALU.add)
                ins.then_inc(sem.row_used, 1)
            dve.wait_ge(sem.row_used, gather_count(l, t, table, 128))
            if table == 0:
                dve.nop().then_inc(sem.dots_ready, 1)
                cnt.next("dots_ready given")
                dve.wait_ge(sem.gelu_ready, cnt.next("gelu_ready"))
                dve.tensor_tensor(k.hdot, k.hdot, k.gate[:, t].rearrange("p h k -> p (h k)"), ALU.mult).then_inc(sem.dve_done, 1)
                dve.wait_ge(sem.dve_done, cnt.next("dve_done"))
    dve.nop().then_inc(sem.experts_summed, 1)
    cnt.next("experts_summed given")
    for j in range(4):
        dve.wait_ge(sem.dve_bank_filled, cnt.next("dve_bank"))
        bank = k.bank["dve"][(cnt["dve_bank"] - 1) % BANKS]
        x = k.x2[:, 2 * j:2 * j + 2, :]
        dve.tensor_tensor(x, bank.rearrange("p (c n) -> p c n", c=2), x, ALU.add).then_inc(sem.dve_bank_free, 1)
    dve.wait_ge(sem.dve_bank_free, BANKS + cnt["dve_bank"])


def peer_pool(pool, cnt, sem, k, l):
    slots = len(k.gather)
    for t in range(2):
        pool.wait_ge(sem.experts_ready, cnt.next("experts_ready"))
        for table, src in enumerate((k.a["peer_u_2"], k.a["peer_v_2"])):
            rows = src.rearrange("l e d -> (l e) d")
            for j in range(128):
                n = gather_count(l, t, table, j)
                if n >= slots:
                    pool.wait_ge(sem.row_used, n - slots + 1)
                pool.indirect_dma_start(k.gather[n % slots], None, rows,
                                          bass.IndirectOffsetOnAxis(ap=k.expert[:, t, j:j + 1], axis=0)
                                          ).then_inc(sem.row_gathered[n % slots], 16)


class Semaphores:

    def __init__(self, nc, ctx):
        self.act_bank_filled = ctx.enter_context(nc.semaphore("act_bank_filled"))
        self.act_bank_free = ctx.enter_context(nc.semaphore("act_bank_free"))
        self.dve_bank_filled = ctx.enter_context(nc.semaphore("dve_bank_filled"))
        self.dve_bank_free = ctx.enter_context(nc.semaphore("dve_bank_free"))
        self.act_done = ctx.enter_context(nc.semaphore("act_done"))
        self.dve_done = ctx.enter_context(nc.semaphore("dve_done"))
        self.pool_done = ctx.enter_context(nc.semaphore("pool_done"))
        self.panel_used = ctx.enter_context(nc.semaphore("panel_used"))
        self.start_loaded = ctx.enter_context(nc.semaphore("start_loaded"))
        self.tables2_loaded = ctx.enter_context(nc.semaphore("tables2_loaded"))
        self.rows2_loaded = ctx.enter_context(nc.semaphore("rows2_loaded"))
        self.squares_ready = ctx.enter_context(nc.semaphore("squares_ready"))
        self.mean_square_ready = ctx.enter_context(nc.semaphore("mean_square_ready"))
        self.root_ready = ctx.enter_context(nc.semaphore("root_ready"))
        self.cond_ready = ctx.enter_context(nc.semaphore("cond_ready"))
        self.xn_ready = ctx.enter_context(nc.semaphore("xn_ready"))
        self.p_ready = ctx.enter_context(nc.semaphore("p_ready"))
        self.rope_ready = ctx.enter_context(nc.semaphore("rope_ready"))
        self.lam_dots_ready = ctx.enter_context(nc.semaphore("lam_dots_ready"))
        self.lam_exp_ready = ctx.enter_context(nc.semaphore("lam_exp_ready"))
        self.lam_row_ready = ctx.enter_context(nc.semaphore("lam_row_ready"))
        self.weights_ready = ctx.enter_context(nc.semaphore("weights_ready"))
        self.neg_max_ready = ctx.enter_context(nc.semaphore("neg_max_ready"))
        self.exp_ready = ctx.enter_context(nc.semaphore("exp_ready"))
        self.att_ready = ctx.enter_context(nc.semaphore("att_ready"))
        self.gates_ready = ctx.enter_context(nc.semaphore("gates_ready"))
        self.lbdiff_ready = ctx.enter_context(nc.semaphore("lbdiff_ready"))
        self.attention_over = ctx.enter_context(nc.semaphore("attention_over"))
        self.diagonal_ready = ctx.enter_context(nc.semaphore("diagonal_ready"))
        self.forward_factors_ready = ctx.enter_context(nc.semaphore("forward_factors_ready"))
        self.backward_factors_ready = ctx.enter_context(nc.semaphore("backward_factors_ready"))
        self.forward_total_ready = ctx.enter_context(nc.semaphore("forward_total_ready"))
        self.tile_states_ready = ctx.enter_context(nc.semaphore("tile_states_ready"))
        self.masks_loaded = ctx.enter_context(nc.semaphore("masks_loaded"))
        self.rec_ready = ctx.enter_context(nc.semaphore("rec_ready"))
        self.silu_ready = ctx.enter_context(nc.semaphore("silu_ready"))
        self.mix_ready = ctx.enter_context(nc.semaphore("mix_ready"))
        self.up_ready = ctx.enter_context(nc.semaphore("up_ready"))
        self.up_used = ctx.enter_context(nc.semaphore("up_used"))
        self.conv_ready = ctx.enter_context(nc.semaphore("conv_ready"))
        self.gate_ready = ctx.enter_context(nc.semaphore("gate_ready"))
        self.hidden_ready = ctx.enter_context(nc.semaphore("hidden_ready"))
        self.block1_done = ctx.enter_context(nc.semaphore("block1_done"))
        self.stored = ctx.enter_context(nc.semaphore("stored"))
        self.out_ready = ctx.enter_context(nc.semaphore("out_ready"))
        self.shifted_ready = ctx.enter_context(nc.semaphore("shifted_ready"))
        self.lora_in_ready = ctx.enter_context(nc.semaphore("lora_in_ready"))
        self.lora_ready = ctx.enter_context(nc.semaphore("lora_ready"))
        self.lora_loaded = ctx.enter_context(nc.semaphore("lora_loaded"))
        self.bonus_ready = ctx.enter_context(nc.semaphore("bonus_ready"))
        self.cum_ready = ctx.enter_context(nc.semaphore("cum_ready"))
        self.decays_ready = ctx.enter_context(nc.semaphore("decays_ready"))
        self.factors_ready = ctx.enter_context(nc.semaphore("factors_ready"))
        self.tri_ready = ctx.enter_context(nc.semaphore("tri_ready"))
        self.state_in_ready = ctx.enter_context(nc.semaphore("state_in_ready"))
        self.rhs_ready = ctx.enter_context(nc.semaphore("rhs_ready"))
        self.sa_ready = ctx.enter_context(nc.semaphore("sa_ready"))
        self.y_ready = ctx.enter_context(nc.semaphore("y_ready"))
        self.rwkv_ready = ctx.enter_context(nc.semaphore("rwkv_ready"))
        self.rel_loaded = ctx.enter_context(nc.semaphore("rel_loaded"))
        self.rel_ready = ctx.enter_context(nc.semaphore("rel_ready"))
        self.line_ready = ctx.enter_context(nc.semaphore("line_ready"))
        self.line_stored = ctx.enter_context(nc.semaphore("line_stored"))
        self.bias_loaded = ctx.enter_context(nc.semaphore("bias_loaded"))
        self.pe_loaded = ctx.enter_context(nc.semaphore("pe_loaded"))
        self.w2_loaded = ctx.enter_context(nc.semaphore("w2_loaded"))
        self.sinks_loaded = ctx.enter_context(nc.semaphore("sinks_loaded"))
        self.pecol_ready = ctx.enter_context(nc.semaphore("pecol_ready"))
        self.blocks_zeroed = ctx.enter_context(nc.semaphore("blocks_zeroed"))
        self.blocks_ready = ctx.enter_context(nc.semaphore("blocks_ready"))
        self.hidden_read = ctx.enter_context(nc.semaphore("hidden_read"))
        self.nsa_keys_ready = ctx.enter_context(nc.semaphore("nsa_keys_ready"))
        self.merged_ready = ctx.enter_context(nc.semaphore("merged_ready"))
        self.square_chunk_ready = ctx.enter_context(nc.semaphore("square_chunk_ready"))
        self.normalised_chunk_ready = ctx.enter_context(nc.semaphore("normalised_chunk_ready"))
        self.attention2_ready = ctx.enter_context(nc.semaphore("attention2_ready"))
        self.ada_ready = ctx.enter_context(nc.semaphore("ada_ready"))
        self.head_scores_ready = ctx.enter_context(nc.semaphore("head_scores_ready"))
        self.token_rows_ready = ctx.enter_context(nc.semaphore("token_rows_ready"))
        self.best_ready = ctx.enter_context(nc.semaphore("best_ready"))
        self.gate_exp_ready = ctx.enter_context(nc.semaphore("gate_exp_ready"))
        self.dots_ready = ctx.enter_context(nc.semaphore("dots_ready"))
        self.gelu_ready = ctx.enter_context(nc.semaphore("gelu_ready"))
        self.experts_ready = ctx.enter_context(nc.semaphore("experts_ready"))
        self.experts_summed = ctx.enter_context(nc.semaphore("experts_summed"))
        self.row_used = ctx.enter_context(nc.semaphore("row_used"))
        self.vectors_ready = ctx.enter_context(nc.semaphore("vectors_ready"))
        self.rows_cleared = ctx.enter_context(nc.semaphore("rows_cleared"))
        self.panel_loaded = [ctx.enter_context(nc.semaphore(f"panel_loaded{i}")) for i in range(RING)]
        self.row_gathered = [ctx.enter_context(nc.semaphore(f"row_gathered{i}")) for i in range(ROWS)]


class Plan:
    pass


def network_kernel(nc, a):
    k = Plan()
    k.a = a
    k.panels, k.panel_value = weight_panels(a), panel_values(a)
    k.hgrn_bank = {}
    k.score_bank = {}
    line_dram = nc.dram_tensor("bias_line", (2, 8, 384), F32, kind="Internal")
    with ExitStack() as ctx:
        sem = Semaphores(nc, ctx)
        sb = lambda name, n: ctx.enter_context(nc.sbuf_tensor(name, [P, n], F32))[:, :]
        banks = [ctx.enter_context(nc.psum_tensor(f"bank{i}", [P, 512], F32))[:, :] for i in range(8)]
        k.bank = {"act": banks[0:4], "dve": banks[4:8]}
        k.ring = sb("ring", RING * 2048)
        tables = sb("tables", max(T1_W, T2_W))
        k.vec = sb("vec", VEC_W)
        main = sb("main", 20480)
        xreg = sb("xreg", 4096)
        scratch = sb("scratch", 11776)
        misc = sb("misc", 1900)

        def cut(base, start, *dims):
            n = 1
            for x in dims:
                n *= x
            ap = base[:, start:start + n]
            if len(dims) == 1:
                return ap
            letters = "abcd"[:len(dims)]
            return ap.rearrange(f"p ({' '.join(letters)}) -> p {' '.join(letters)}",
                                **{c: d for c, d in zip(letters[:-1], dims[:-1])})

        k.c1 = {n: tables[:, o:o + w] for n, (o, w) in T1.items()}
        k.c2 = {n: tables[:, o:o + w] for n, (o, w) in T2.items()}
        k.ident, k.ones = k.c1["ident"], k.c1["ones"]
        k.v1 = lambda l, n: k.vec[:, PACK1[l] + V1[n][0]:PACK1[l] + V1[n][0] + V1[n][1]]
        k.v2 = lambda l, n: k.vec[:, PACK2[l] + V2[n][0]:PACK2[l] + V2[n][0] + V2[n][1]]

        def conv(l, tap, c):
            col = PACKC[l][tap // 2] + 44 * (tap % 2) + c
            return k.vec[:, col:col + 1]
        k.conv = conv
        k.panel = lambda i, cols=PANEL: k.ring[:, (i % RING) * 2048:(i % RING) * 2048 + 2048 // cols * cols].rearrange(
            "p (c n) -> p c n", n=cols)
        k.x, k.xn, k.p = cut(main, 0, 8, 512), cut(main, 4096, 8, 512), cut(main, 8192, 24, 512)
        k.h = cut(main, 8192, 22, 512)
        k.mix = cut(xreg, 0, 8, 512)
        k.tokens = cut(main, 8192, 4, 1024)
        k.rows = scratch[:, 0:1024]
        k.vt, k.e, k.et = cut(scratch, 0, 4, 512), cut(scratch, 2048, 2, 2, 512), cut(scratch, 4096, 2, 4, 128)
        k.o, k.sq, k.hk = cut(scratch, 5120, 4, 512), cut(scratch, 7168, 4, 512), cut(scratch, 9216, 4, 512)
        k.fa, k.fy = cut(scratch, 2048, 4, 2, 256), cut(scratch, 4096, 2, 512)
        k.hq, k.ksum, k.hvt = cut(scratch, 0, 4, 512), cut(scratch, 2048, 2, 512), cut(scratch, 3072, 4, 256)
        k.hkt, k.hsin = cut(scratch, 4096, 2, 4, 256), scratch[:, 6144:8192].rearrange(
            "p (d t g n) -> p d t g n", d=2, t=4, g=2)
        k.ha = main[:, 4096:6144].rearrange("p (a b j n) -> p a b j n", a=2, b=2, j=4)
        k.hmask = cut(main, 6144, 2, 7, 128)
        k.hdel = main[:, 8192:10240].rearrange("p (d t j n) -> p d t j n", d=2, t=2, j=4)
        k.tmp = scratch[:, 11264:11776]
        k.u, k.cv = cut(scratch, 0, 2, 4, 512), cut(scratch, 4096, 2, 4, 512)
        k.mod, k.modw, k.cond = cut(misc, 0, 48, 2), cut(misc, 96, 2, 8, 2), cut(misc, 128, 8, 2)
        k.stat, k.neglam, k.lamsum = cut(misc, 1744, 2, 8), misc[:, 152:153], misc[:, 153:157]
        k.modraw, k.adarow = cut(misc, 1760, 48, 2), cut(misc, 1196, 2, PANEL)
        k.lbdiff, k.lbd, k.oml = misc[:, 160:164], misc[:, 164:168], misc[:, 168:172]
        k.rms, k.lamrow = misc[:, 172:684], misc[:, 684:1196]
        k.x2, k.xn2 = cut(xreg, 0, 8, 256), cut(xreg, 2048, 8, 256)
        k.p2 = cut(main, 0, 55, 256)
        s4 = lambda i: cut(scratch, i * 1024, 4, 256)
        k.shift = cut(scratch, 5120, 14, 256)
        k.lw, k.ap, k.bi, k.g, k.bonus, k.ra = s4(0), s4(1), s4(2), s4(3), s4(4), s4(5)
        k.tb, k.tk, k.tv = (cut(scratch, 6144 + 1024 * i, 2, 512) for i in range(3))
        k.xf = cut(scratch, 9216, 2, 4, 128)
        k.aak = cut(scratch, 10240, 2, 4, 128)
        k.arb, k.ark = cut(main, 14080, 2, 4, 128), cut(main, 15104, 2, 4, 128)
        k.e1, k.e2 = cut(scratch, 6144, 4, 256), cut(scratch, 7168, 4, 256)
        k.tri_m = cut(main, 16128, 4, 128), cut(misc, 684, 4, 128)
        k.tri_b = cut(main, 16640, 4, 128), cut(misc, 1196, 4, 128)
        k.tri_n = cut(main, 17152, 4, 128), cut(misc, 172, 4, 128)
        k.tri_t = cut(main, 17664, 4, 128), cut(main, ZWA * SEQ, 4, 128)
        k.tri_raw = cut(main, 18176, 4, 128), cut(scratch, 11264, 4, 128)
        k.rhs, k.sa, k.st = cut(main, 18688, 512), cut(main, 19200, 512), cut(main, 19712, 4, 128)
        k.lora = cut(misc, 684, 2, 512)
        k.small = misc[:, 0:24]
        k.stat2, k.sinks, k.rel = cut(misc, 1708, 3, 12), misc[:, 36:44], misc[:, 44:60]
        k.gt, k.cmadd = cut(misc, 60, 2, 24), misc[:, 108:140]
        k.bias = cut(scratch, 0, 2, 8, 256)
        k.kp = cut(scratch, 4096, 3, 4, 256)
        k.vtt, k.vcp = cut(scratch, 7168, 3, 2, 128), cut(scratch, 7936, 128)
        k.kcp, k.pecol, k.hid = cut(scratch, 8064, 2, 2, 16), cut(scratch, 8128, 2, 32), cut(scratch, 8192, 2, 32)
        k.perow = cut(scratch, 8256, 2, 128)
        k.cw2 = cut(scratch, 8512, 2, 2, 64)
        k.ew, k.line = cut(scratch, 8832, 3, 896), cut(scratch, 8832, 2, 384)
        k.zz, k.zzflat = cut(main, 18176, 2, 2, 256), main[:, 18176:19200]
        k.flipped = cut(main, 14080, 2, 2048)
        k.hidrow = scratch[:, 11520:11776]
        k.ewt = cut(main, 14080, 2, 7, 128)
        k.merged, k.btmp = cut(scratch, 0, 8, 256), cut(scratch, 2048, 2, 256)
        k.pq, k.zt, k.skt = cut(main, 0, 16, 256), cut(main, 4096, 2, 1024), cut(main, 6144, 16, 128)
        k.ps = cut(main, 8192, 2, 16, 128)
        k.gather = [main[:, 12288 + 1024 * i:13312 + 1024 * i] for i in range(ROWS)]
        k.acc = cut(main, 18432, 2, 1024)
        k.tv16, k.tif = cut(scratch, 0, 16, 16), cut(scratch, 256, 16, 16)
        k.cand, k.gate = scratch[:, 512:768], cut(scratch, 1552, 2, 8, 16)
        k.rankf, k.key = cut(scratch, 896, 2, 8, 16), cut(scratch, 1152, 2, 128)
        k.hdot, k.gmax = scratch[:, 1408:1536], scratch[:, 1536:1544]
        k.hot = cut(scratch, 2048, 128, 16)
        ints = ctx.enter_context(nc.sbuf_tensor("ints", [P, 896], U32))[:, :]
        k.ti16, k.flat = cut(ints, 0, 16, 16), cut(ints, 256, 8, 16)
        k.rank, k.expert = cut(ints, 384, 2, 8, 16), cut(ints, 640, 2, 128)
        k.outbuf = cut(scratch, 4096, 2, 1024)

        block = ctx.enter_context(nc.Block())

        @block.sync
        def _(sp):
            cnt = Counts()
            start = sem.start_loaded

            def row(dst0, src, rows):
                sp.dma_start(k.rows[dst0[0]:dst0[0] + rows, dst0[1]:dst0[1] + P], src).then_inc(start, 16)
                k.start += 16
            k.start = 0
            sp.dma_start(tables[:, 0:T1_W], a["tables1"]).then_inc(start, 16)
            sp.dma_start(k.tokens[:, 0:2, :], a["ctx"][0].rearrange("(t p) d -> p t d", p=P)).then_inc(start, 16)
            sp.dma_start(k.tokens[:, 2:4, :], a["x"][0].rearrange("(t p) d -> p t d", p=P)).then_inc(start, 16)
            sp.dma_start(k.lamrow[0:1, 0:512], a["lam_qk"].rearrange("l a d -> (l a d)").unsqueeze(0)).then_inc(start, 16)
            k.start += 64
            sp.wait_ge(sem.rows_cleared, 1)
            r128 = lambda v: v.rearrange("(c p) -> c p", p=P)
            for l in range(DEPTH):
                put = lambda name, v, rows, off=0: row((V1[name][0] + off, PACK1[l]), v, rows)
                put("norm1", r128(a["norm1_w"][l]), 8)
                put("norm2", r128(a["norm2_w"][l]), 8)
                put("subln", a["subln_w"][l].unsqueeze(0), 1)
                for half in range(2):
                    sp.dma_start(k.rows[V1["hnorm"][0]:V1["hnorm"][0] + 1, PACK1[l] + half * 64:PACK1[l] + half * 64 + 64],
                                 a["hgrn_norm_w"][l].unsqueeze(0)).then_inc(start, 16)
                k.start += 32
                put("lb", a["lb_param"].rearrange("l s (c p) -> (l s c) p", p=P), 8)
                put("b_ada", r128(a["b_ada"][l]), 48)
                put("cond", r128(a["c_ctx"]), 8)
                put("cond", r128(a["c"][0]), 8, 8)
                put("final", r128(a["final_norm_w"]), 8)
                for tap in range(4):
                    v = a["conv_w"][l, tap] if tap < 3 else a["conv_b"][l]
                    row((44 * (tap % 2), PACKC[l][tap // 2]), r128(v), 44)
                put = lambda name, v: row((V2[name][0], PACK2[l]), v, V2[name][1])
                for name, v in (("ln1", a["ln1_w_2"][l]), ("ln2", a["ln2_w_2"][l]), ("mu", a["rwkv_mu_2"][l]),
                                ("w0", a["rwkv_w0_2"][l]), ("a0", a["rwkv_a0_2"][l]), ("kk", a["rwkv_k_k_2"][l]),
                                ("ka", a["rwkv_k_a_2"][l]), ("rk", a["rwkv_r_k_2"][l].rearrange("h d -> (h d)")),
                                ("lnw", a["rwkv_ln_w_2"][l]), ("lnb", a["rwkv_ln_b_2"][l]), ("lnf", a["lnf_w_2"])):
                    put(name, r128(v))
            load_panels(sp, cnt, sem, k)
            sp.wait_ge(sem.out_ready, 1)
            sp.dma_start(a["out"][0].rearrange("(t p) d -> p t d", p=P), k.outbuf[:, :, :]).then_inc(sem.stored, 16)
            sp.wait_ge(sem.stored, 16)

        packs = [(c, None) for c in (PACK1[0], PACK1[1], PACKC[0][0], PACKC[0][1], PACKC[1][0], PACKC[1][1],
                                     PACK2[0], PACK2[1])]

        @block.tensor
        def _(pe):
            cnt = Counts()
            pe.wait_ge(sem.start_loaded, k.start)
            vectors_to_columns_tensor(pe, cnt, sem, k, packs)
            tokens_to_features_tensor(pe, cnt, sem, k, k.tokens, 4)
            pe.wait_ge(sem.act_bank_free, BANKS + cnt["act_bank"])
            pe.wait_ge(sem.cond_ready, cnt.next("cond_ready"))
            ada_tensor(pe, cnt, sem, k, (0, ADA_STEPS))
            for l in range(DEPTH):
                tok = (tokens_of(l), TOK)
                norm_tensor(pe, cnt, sem, k, (0, TOK))
                project_tensor(pe, cnt, sem, k, l)
                lambda_tensor(pe, cnt, sem, k)
                rope_tensor(pe, cnt, sem, k)
                values_tensor(pe, cnt, sem, k)
                fourier_tensor(pe, cnt, sem, k, l)
                k.score_bank[l] = cnt["dve_bank"]
                attention_tensor(pe, cnt, sem, k, l)
                hgrn_tensor(pe, cnt, sem, k, l)
                group_norm_tensor(pe, cnt, sem, k, k.sq[:, :, tok[0]:TOK], 2, TOK - tok[0], k.c1["block"])
                merge_tensor(pe, cnt, sem, k, l)
                norm_tensor(pe, cnt, sem, k, tok)
                ffn_up_tensor(pe, cnt, sem, k, l)
                ffn_down_tensor(pe, cnt, sem, k, l)
            norm_tensor(pe, cnt, sem, k, (CTX, TOK))
            pe.wait_ge(sem.tables2_loaded, 16)
            bias_line_tensor(pe, cnt, sem, k)
            for l in range(DEPTH):
                norm_tensor(pe, cnt, sem, k, (0, SEQ), k.xn2)
                project2_tensor(pe, cnt, sem, k, RWKV_STEPS)
                project2_tensor(pe, cnt, sem, k, LORA_STEPS)
                rwkv_inputs_tensor(pe, cnt, sem, k, l)
                rwkv_solve_tensor(pe, cnt, sem, k)
                nsa_prepare_tensor(pe, cnt, sem, k, l)
                attention2_tensor(pe, cnt, sem, k, l)
                branches_tensor(pe, cnt, sem, k, l)
                norm_tensor(pe, cnt, sem, k, (0, SEQ), k.xn2)
                peer_tensor(pe, cnt, sem, k, l)
            norm_tensor(pe, cnt, sem, k, (0, SEQ), k.xn2)
            pe.wait_ge(sem.xn_ready, cnt.next("xn_ready", DC))
            store_features_tensor(pe, cnt, sem, k, k.xn2)

        @block.scalar
        def _(act):
            cnt = Counts()
            act.nop().then_inc(sem.act_bank_free, BANKS)
            vectors_to_columns_scalar(act, cnt, sem, k, packs)
            for c in range(DC):
                act.wait_ge(sem.act_bank_filled, cnt.next("act_bank"))
                bank = k.bank["act"][(cnt["act_bank"] - 1) % BANKS]
                act.activation(k.x[:, c, :], bank, ACT.Copy).then_inc(sem.act_bank_free, 1)
            cond_stage_scalar(act, cnt, sem, k)
            act.nop().then_inc(sem.vectors_ready, 1)
            cnt.next("vectors_ready given")
            ada_scalar(act, cnt, sem, k, (0, ADA_STEPS))
            for l in range(DEPTH):
                t0 = tokens_of(l)
                root_scalar(act, cnt, sem, k, k.rms[:, 0:TOK])
                modulate_scalar(act, cnt, sem, k, 0, 0)
                lambda_scalar(act, cnt, sem, k)
                project_scalar(act, cnt, sem, k, l)
                values_scalar(act, cnt, sem, k)
                fourier_scalar(act, cnt, sem, k, l)
                if l > 0:
                    act.wait_ge(sem.lbdiff_ready, cnt.next("lbdiff_ready"))
                attention_scalar(act, cnt, sem, k, l)
                hgrn_scalar(act, cnt, sem, k, l)
                hgrn_out_scalar(act, cnt, sem, k, l)
                root_scalar(act, cnt, sem, k, k.sq[:, 0:2, t0:TOK])
                root_scalar(act, cnt, sem, k, k.rms[:, 0:TOK - t0])
                modulate_scalar(act, cnt, sem, k, 1, t0)
                ffn_up_scalar(act, cnt, sem, k, l)
            root_scalar(act, cnt, sem, k, k.rms[:, 0:SEQ])
            act.wait_ge(sem.block1_done, cnt.next("block1_done"))
            act.dma_start(tables[:, 0:T2_W], a["tables2"]).then_inc(sem.tables2_loaded, 16)
            act.dma_start(k.rel[0:32, :], a["rel_bias_2"]).then_inc(sem.rel_loaded, 16)
            bias_line_scalar(act, cnt, sem, k)
            act.dma_start(line_dram.ap().rearrange("s h n -> h s n"), k.line[0:8]).then_inc(sem.line_stored, 16)
            act.wait_ge(sem.line_stored, 16)
            for l in range(DEPTH):
                act.dma_start(k.lora[0:64, 0, :], a["rwkv_w2_2"][l]).then_inc(sem.lora_loaded, 16)
                act.dma_start(k.lora[64:128, 0, :], a["rwkv_a2_2"][l]).then_inc(sem.lora_loaded, 16)
                act.dma_start(k.lora[:, 1, :], a["rwkv_g2_2"][l]).then_inc(sem.lora_loaded, 16)
                act.dma_start(k.sinks, a["swa_sinks_2"][l:l + 1, :].to_broadcast([P, 8])).then_inc(sem.sinks_loaded, 16)
                root_scalar(act, cnt, sem, k, k.rms[:, 0:SEQ])
                project2_scalar(act, cnt, sem, k, RWKV_STEPS)
                act.wait_ge(sem.act_bank_free, BANKS + cnt["act_bank"])
                act.nop().then_inc(sem.p_ready, 1)
                cnt.next("p_ready given")
                project2_scalar(act, cnt, sem, k, LORA_STEPS)
                rwkv_inputs_scalar(act, cnt, sem, k, l)
                project2_scalar(act, cnt, sem, k, SOLVE_STEPS)
                root_scalar(act, cnt, sem, k, k.ra)
                for kind in range(2):
                    src = bass.AP(line_dram, kind * 8 * 384, [[1, P], [384, 8], [1, 256]])
                    act.dma_start(k.flipped[:, kind, :].rearrange("p (h n) -> p h n", h=8), src
                                  ).then_inc(sem.bias_loaded, 16)
                    act.wait_ge(sem.bias_loaded, 16 * (2 * l + kind + 1))
                for kind, (pos, w2) in enumerate(((a["nsa_pe_k_2"][l], a["nsa_ck_w2_2"][l]), (a["nsa_pe_v_2"][l], a["nsa_cv_w2_2"][l]))):
                    for half in range(2):
                        act.dma_start(k.perow[0:32, kind, half * 64:half * 64 + 64], pos).then_inc(sem.pe_loaded, 16)
                    act.dma_start(k.cw2[:, kind, :, :], w2.rearrange("(c p) n -> p c n", p=P)).then_inc(sem.w2_loaded, 16)
                    act.wait_ge(sem.w2_loaded, 16 * (2 * l + kind + 1))
                act.wait_ge(sem.rwkv_ready, cnt.next("rwkv_ready"))
                nsa_prepare_scalar(act, cnt, sem, k, l)
                attention2_scalar(act, cnt, sem, k, l)
                root_scalar(act, cnt, sem, k, k.rms[:, 0:SEQ])
                peer_scalar(act, cnt, sem, k, l)
            root_scalar(act, cnt, sem, k, k.rms[:, 0:SEQ])
            store_features_scalar(act, cnt, sem, k, k.outbuf)
            act.nop().then_inc(sem.out_ready, 1)
            cnt.next("out_ready given")

        @block.vector
        def _(dve):
            cnt = Counts()
            dve.nop().then_inc(sem.dve_bank_free, BANKS)
            dve.memset(k.rows, 0.0).then_inc(sem.rows_cleared, 1)
            dve.wait_ge(sem.rows_cleared, cnt.next("rows_cleared given"))
            dve.wait_ge(sem.vectors_ready, cnt.next("vectors_ready"))
            lower_bound_vector(dve, cnt, sem, k)
            for l in range(DEPTH):
                t0 = tokens_of(l)
                ada_vector(dve, cnt, sem, k, l)
                norm_vector(dve, cnt, sem, k, k.x, (0, TOK))
                normalise_vector(dve, cnt, sem, k, (0, TOK))
                lambda_vector(dve, cnt, sem, k, l)
                rope_vector(dve, cnt, sem, k)
                attention_vector(dve, cnt, sem, k, l)
                hgrn_gates_vector(dve, cnt, sem, k, l)
                hgrn_vector(dve, cnt, sem, k, l)
                hgrn_out_vector(dve, cnt, sem, k, l)
                dve.nop().then_inc(sem.mix_ready, 1)
                cnt.next("mix_ready given")
                residual_vector(dve, cnt, sem, k, l, 16)
                norm_vector(dve, cnt, sem, k, k.x, (t0, TOK))
                normalise_vector(dve, cnt, sem, k, (t0, TOK))
                ffn_up_vector(dve, cnt, sem, k, l)
                residual_vector(dve, cnt, sem, k, l, 40)
            norm_vector(dve, cnt, sem, k, k.x, (CTX, TOK))
            for c in range(DC):
                ins = dve.scalar_tensor_tensor(k.x2[:, c, :], k.x[:, c, CTX:TOK], k.v1(0, "final")[:, c:c + 1],
                                               k.rms[:, 0:SEQ], ALU.mult, ALU.mult)
            ins.then_inc(sem.dve_done, 1)
            dve.wait_ge(sem.dve_done, cnt.next("dve_done"))
            dve.memset(k.rel[32:64, :], NEG).then_inc(sem.rel_ready, 1)
            dve.wait_ge(sem.rel_ready, cnt.next("rel_ready given"))
            dve.nop().then_inc(sem.block1_done, 1)
            cnt.next("block1_done given")
            for l in range(DEPTH):
                norm2_vector(dve, cnt, sem, k, l, "ln1")
                rwkv_inputs_vector(dve, cnt, sem, k, l)
                rwkv_solve_vector(dve, cnt, sem, k, l)
                nsa_prepare_vector(dve, cnt, sem, k, l)
                attention2_vector(dve, cnt, sem, k, l)
                branches_vector(dve, cnt, sem, k, l)
                norm2_vector(dve, cnt, sem, k, l, "ln2")
                peer_vector(dve, cnt, sem, k, l)
            norm2_vector(dve, cnt, sem, k, 0, "lnf")

        @block.gpsimd
        def _(pool):
            cnt = Counts()
            for l in range(DEPTH):
                hgrn_pool(pool, cnt, sem, k, l)
            for l in range(DEPTH):
                peer_pool(pool, cnt, sem, k, l)


_INS = ["x", "c", "ctx", "c_ctx", "w_ada", "b_ada", "norm1_w", "norm2_w", "w_in", "lam_qk", "subln_w", "lb_param",
        "hgrn_norm_w", "w_fnet", "w_out", "w_up", "conv_w", "conv_b", "w_down", "final_norm_w", "ln1_w_2", "ln2_w_2",
        "lnf_w_2", "rel_bias_2", "w_in_2", "rwkv_mu_2", "rwkv_w0_2", "rwkv_w2_2", "rwkv_a0_2", "rwkv_a2_2",
        "rwkv_g2_2", "rwkv_k_k_2", "rwkv_k_a_2", "rwkv_r_k_2", "rwkv_ln_w_2", "rwkv_ln_b_2", "nsa_pe_k_2",
        "nsa_pe_v_2", "nsa_ck_w1_2", "nsa_ck_w2_2", "nsa_cv_w1_2", "nsa_cv_w2_2", "swa_sinks_2", "w_br_a_2",
        "w_br_b_2", "w_br_c_2", "w_out_2", "peer_wq_2", "peer_subkeys_2", "peer_u_2", "peer_v_2"]


def kernel(**inputs):
    import concourse.bacc as bacc
    from concourse.bass_utils import run_bass_kernel_spmd

    nc = bacc.Bacc("TRN2", target_bir_lowering=False, num_devices=1)
    arrays = {n: np.ascontiguousarray(inputs[n]) for n in _INS}
    arrays["tables1"], arrays["tables2"] = constant_tables()
    arrays["masks"] = recurrence_masks()
    a = {n: nc.dram_tensor(f"in_{n}", v.shape, mybir.dt.from_np(v.dtype), kind="ExternalInput").ap()
         for n, v in arrays.items()}
    a["out"] = nc.dram_tensor("out_0", (1, SEQ, D), F32, kind="ExternalOutput").ap()
    network_kernel(nc, a)
    r = run_bass_kernel_spmd(nc, [{f"in_{n}": v for n, v in arrays.items()}], core_ids=[0])
    return r.results[0]["out_0"]
```
